# Optimizing a Trainium2 kernel written in Bass

```python
import math
import jax
import jax.numpy as jnp
from jax import lax
import numpy as np

D_MODEL = 1024
BATCH = 1
SEQ = 1024
DEPTH = 2

CHUNK = 64
Q_BLOCK = 128
N_MIXERS = 3
EPS = 1e-6
NEG_INF = -1e30
D_FF = 4 * D_MODEL
N_MOD = 6

GLA_HEADS = 4
GLA_DK = D_MODEL // (2 * GLA_HEADS)
GLA_DV = D_MODEL // GLA_HEADS
GLA_GATE_RANK = 16
GLA_GATE_TEMP = 16.0
GLA_KW = GLA_HEADS * GLA_DK
GLA_VW = GLA_HEADS * GLA_DV
GLA_IN = 2 * GLA_KW + 2 * GLA_VW + GLA_GATE_RANK
GLA_SPLITS = [GLA_KW, 2 * GLA_KW, 2 * GLA_KW + GLA_VW, 2 * GLA_KW + 2 * GLA_VW]

MLA_HEADS = 16
MLA_NOPE = 64
MLA_ROPE = 32
MLA_V = 64
MLA_Q_RANK = 384
MLA_KV_RANK = 256
MLA_IN = MLA_Q_RANK + MLA_KV_RANK + MLA_ROPE
ROPE_THETA = 10000.0

GDN_K_HEADS = 8
GDN_V_HEADS = 16
GDN_DK = 128
GDN_DV = 128
GDN_CONV = 4
GDN_QKW = GDN_K_HEADS * GDN_DK
GDN_VW = GDN_V_HEADS * GDN_DV
GDN_CONV_W = 2 * GDN_QKW + GDN_VW
GDN_IN = GDN_CONV_W + GDN_VW + 2 * GDN_V_HEADS
GDN_SPLITS = [GDN_CONV_W, GDN_CONV_W + GDN_VW, GDN_CONV_W + GDN_VW + GDN_V_HEADS]

N_GLA = len(range(0, DEPTH, N_MIXERS))
N_MLA = len(range(1, DEPTH, N_MIXERS))
N_GDN = len(range(2, DEPTH, N_MIXERS))

kernel_name = "chunk_causal_hybrid_gla_mla_gdn_trunk"

def rms_norm(x, g):
    xf = x.astype(jnp.float32)
    y = xf * lax.rsqrt(jnp.mean(xf * xf, axis=-1, keepdims=True) + EPS)
    return (y * g.astype(jnp.float32)).astype(x.dtype)

def l2_normalize(x):
    return x * lax.rsqrt(jnp.sum(x * x, axis=-1, keepdims=True) + EPS)

def to_chunks(t, heads):
    b, s = t.shape[0], t.shape[1]
    return t.reshape(b, s // CHUNK, CHUNK, heads, -1).transpose(1, 0, 3, 2, 4)

def from_chunks(t):
    nc, b, h, l, d = t.shape
    return t.transpose(1, 0, 3, 2, 4).reshape(b, nc * l, h, d)

def gla_mixer(h, w_in, w_gate_up, b_gate, head_g, w_out):
    b, s, _ = h.shape
    f32 = jnp.float32
    q, k, v, r, g_lr = jnp.split(h @ w_in, GLA_SPLITS, axis=-1)
    log_a = jax.nn.log_sigmoid((g_lr @ w_gate_up + b_gate).astype(f32)) / GLA_GATE_TEMP
    qc = to_chunks(q.astype(f32) * GLA_DK ** -0.5, GLA_HEADS)
    kc = to_chunks(k.astype(f32), GLA_HEADS)
    vc = to_chunks(v.astype(f32), GLA_HEADS)
    cum = jnp.cumsum(to_chunks(log_a, GLA_HEADS), axis=3)
    k_end = kc * jnp.exp(cum[..., -1:, :] - cum)
    dec = jnp.exp(cum[..., -1, :])

    def step(state, inp):
        d, ke, vv, qq = inp
        state = d[..., :, None] * state + jnp.einsum('bhlk,bhlv->bhkv', ke, vv)
        return state, jnp.einsum('bhlk,bhkv->bhlv', qq, state)

    s0 = jnp.zeros((b, GLA_HEADS, GLA_DK, GLA_DV), f32)
    _, o = lax.scan(step, s0, (dec, k_end, vc, qc))
    o = rms_norm(from_chunks(o), head_g) * jax.nn.silu(r.astype(f32)).reshape(b, s, GLA_HEADS, GLA_DV)
    return o.reshape(b, s, GLA_VW).astype(h.dtype) @ w_out

def rope_tables(positions):
    half = MLA_ROPE // 2
    inv_freq = ROPE_THETA ** (-jnp.arange(half, dtype=jnp.float32) / half)
    ang = positions.astype(jnp.float32)[..., None] * inv_freq
    return jnp.cos(ang), jnp.sin(ang)

def apply_rope(x, cos, sin):
    x1, x2 = jnp.split(x.astype(jnp.float32), 2, axis=-1)
    return jnp.concatenate([x1 * cos - x2 * sin, x1 * sin + x2 * cos], axis=-1).astype(x.dtype)

def mla_mixer(h, positions, w_in, q_norm_g, w_uq, kv_norm_g, w_ukv, w_out):
    b, s, _ = h.shape
    c_q, c_kv, k_rope = jnp.split(h @ w_in, [MLA_Q_RANK, MLA_Q_RANK + MLA_KV_RANK], axis=-1)
    q = (rms_norm(c_q, q_norm_g) @ w_uq).reshape(b, s, MLA_HEADS, MLA_NOPE + MLA_ROPE)
    kv = (rms_norm(c_kv, kv_norm_g) @ w_ukv).reshape(b, s, MLA_HEADS, MLA_NOPE + MLA_V)
    q_nope, q_rope = jnp.split(q, [MLA_NOPE], axis=-1)
    k_nope, v = jnp.split(kv, [MLA_NOPE], axis=-1)
    cos, sin = rope_tables(positions)
    q_rope = apply_rope(q_rope, cos[:, :, None, :], sin[:, :, None, :])
    k_rope = apply_rope(k_rope, cos, sin)
    scale = (MLA_NOPE + MLA_ROPE) ** -0.5
    n_blk = s // Q_BLOCK
    key_chunk = jnp.arange(s) // CHUNK

    def blocks(t):
        return t.reshape(b, n_blk, Q_BLOCK, MLA_HEADS, -1).transpose(1, 0, 2, 3, 4)

    def attend(args):
        qn, qr, blk = args
        sc = (jnp.einsum('bqhd,bkhd->bhqk', qn, k_nope)
              + jnp.einsum('bqhr,bkr->bhqk', qr, k_rope)).astype(jnp.float32) * scale
        q_chunk = (blk * Q_BLOCK + jnp.arange(Q_BLOCK)) // CHUNK
        mask = key_chunk[None, :] <= q_chunk[:, None]
        p = jax.nn.softmax(jnp.where(mask, sc, NEG_INF), axis=-1).astype(v.dtype)
        return jnp.einsum('bhqk,bkhd->bqhd', p, v)

    o = lax.map(attend, (blocks(q_nope), blocks(q_rope), jnp.arange(n_blk)))
    o = o.transpose(1, 0, 2, 3, 4).reshape(b, s, MLA_HEADS * MLA_V)
    return o @ w_out

def causal_conv(x, w):
    s = x.shape[1]
    xp = jnp.pad(x, ((0, 0), (GDN_CONV - 1, 0), (0, 0)))
    out = xp[:, 0:s] * w[0]
    for j in range(1, GDN_CONV):
        out = out + xp[:, j:j + s] * w[j]
    return out

def gdn_mixer(h, w_in, conv_w, a_log, dt_bias, norm_g, w_out):
    b, s, _ = h.shape
    f32 = jnp.float32
    qkv, z, b_raw, a_raw = jnp.split(h @ w_in, GDN_SPLITS, axis=-1)
    qkv = jax.nn.silu(causal_conv(qkv, conv_w))
    q, k, v = jnp.split(qkv.astype(f32), [GDN_QKW, 2 * GDN_QKW], axis=-1)
    rep = GDN_V_HEADS // GDN_K_HEADS
    q = jnp.repeat(l2_normalize(q.reshape(b, s, GDN_K_HEADS, GDN_DK)), rep, axis=2) * GDN_DK ** -0.5
    k = jnp.repeat(l2_normalize(k.reshape(b, s, GDN_K_HEADS, GDN_DK)), rep, axis=2)
    beta = jax.nn.sigmoid(b_raw.astype(f32))
    g = -jnp.exp(a_log.astype(f32)) * jax.nn.softplus(a_raw.astype(f32) + dt_bias.astype(f32))
    qc = to_chunks(q.reshape(b, s, -1), GDN_V_HEADS)
    kc = to_chunks(k.reshape(b, s, -1), GDN_V_HEADS)
    vc = to_chunks(v, GDN_V_HEADS)
    bc = to_chunks(beta, GDN_V_HEADS)[..., 0]
    cum = jnp.cumsum(to_chunks(g, GDN_V_HEADS)[..., 0], axis=-1)
    strict = jnp.tril(jnp.ones((CHUNK, CHUNK), dtype=bool), -1)
    diff = jnp.where(strict, cum[..., :, None] - cum[..., None, :], 0.0)
    kk = jnp.einsum('nbhik,nbhjk->nbhij', kc, kc)
    a_mat = jnp.where(strict, bc[..., :, None] * jnp.exp(diff) * kk, 0.0)
    lhs = a_mat + jnp.eye(CHUNK, dtype=f32)
    rhs = jnp.concatenate([bc[..., None] * vc, (bc * jnp.exp(cum))[..., None] * kc], axis=-1)
    sol = lax.linalg.triangular_solve(lhs, rhs, left_side=True, lower=True, unit_diagonal=True)
    w_v, w_k = jnp.split(sol, [GDN_DV], axis=-1)
    k_end = kc * jnp.exp(cum[..., -1:] - cum)[..., None]
    dec = jnp.exp(cum[..., -1])

    def step(state, inp):
        wv, wk, ke, d, qq = inp
        u = wv - jnp.einsum('bhlk,bhkv->bhlv', wk, state)
        state = d[..., None, None] * state + jnp.einsum('bhlk,bhlv->bhkv', ke, u)
        return state, jnp.einsum('bhlk,bhkv->bhlv', qq, state)

    s0 = jnp.zeros((b, GDN_V_HEADS, GDN_DK, GDN_DV), f32)
    _, o = lax.scan(step, s0, (w_v, w_k, k_end, dec, qc))
    o = rms_norm(from_chunks(o), norm_g) * jax.nn.silu(z.astype(f32)).reshape(b, s, GDN_V_HEADS, GDN_DV)
    return o.reshape(b, s, GDN_VW).astype(h.dtype) @ w_out

def squared_relu_mlp(h, w_up, w_down):
    return jnp.square(jax.nn.relu(h @ w_up)) @ w_down

def setup_inputs(seed: int = 0) -> dict:
    key = jax.random.key(seed)
    ks = iter(jax.random.split(key, 40))
    f32 = jnp.float32

    def nrm(shape, scale):
        return jax.random.normal(next(ks), shape, f32) * scale

    def gain(shape):
        return 1.0 + nrm(shape, 0.1)

    x = nrm((BATCH, SEQ, D_MODEL), 1.0)
    c = nrm((BATCH, D_MODEL), 1.0)
    positions = jnp.broadcast_to(jnp.arange(SEQ, dtype=jnp.int32), (BATCH, SEQ))
    ada_w = nrm((DEPTH, D_MODEL, N_MOD * D_MODEL), 0.5 * D_MODEL ** -0.5)
    ada_b = nrm((DEPTH, N_MOD * D_MODEL), 0.01)
    norm_pre_g = gain((DEPTH, 2, D_MODEL))
    norm_post_g = gain((DEPTH, 2, D_MODEL))

    gla_w_in = nrm((N_GLA, D_MODEL, GLA_IN), D_MODEL ** -0.5)
    gla_w_gate_up = nrm((N_GLA, GLA_GATE_RANK, GLA_KW), GLA_GATE_RANK ** -0.5)
    gla_b_gate = nrm((N_GLA, GLA_KW), 0.1)
    gla_head_g = gain((N_GLA, GLA_DV))
    gla_w_out = nrm((N_GLA, GLA_VW, D_MODEL), GLA_VW ** -0.5)

    mla_w_in = nrm((N_MLA, D_MODEL, MLA_IN), D_MODEL ** -0.5)
    mla_q_norm_g = gain((N_MLA, MLA_Q_RANK))
    mla_w_uq = nrm((N_MLA, MLA_Q_RANK, MLA_HEADS * (MLA_NOPE + MLA_ROPE)), MLA_Q_RANK ** -0.5)
    mla_kv_norm_g = gain((N_MLA, MLA_KV_RANK))
    mla_w_ukv = nrm((N_MLA, MLA_KV_RANK, MLA_HEADS * (MLA_NOPE + MLA_V)), MLA_KV_RANK ** -0.5)
    mla_w_out = nrm((N_MLA, MLA_HEADS * MLA_V, D_MODEL), (MLA_HEADS * MLA_V) ** -0.5)

    gdn_w_in = nrm((N_GDN, D_MODEL, GDN_IN), D_MODEL ** -0.5)
    gdn_conv_w = nrm((N_GDN, GDN_CONV, GDN_CONV_W), GDN_CONV ** -0.5)
    gdn_a_log = jnp.log(jax.random.uniform(next(ks), (N_GDN, GDN_V_HEADS), f32, 1.0, 16.0))
    dt = jnp.exp(jax.random.uniform(next(ks), (N_GDN, GDN_V_HEADS), f32, math.log(1e-3), math.log(1e-1)))
    gdn_dt_bias = dt + jnp.log(-jnp.expm1(-dt))
    gdn_norm_g = gain((N_GDN, GDN_DV))
    gdn_w_out = nrm((N_GDN, GDN_VW, D_MODEL), GDN_VW ** -0.5)

    mlp_w_up = nrm((DEPTH, D_MODEL, D_FF), D_MODEL ** -0.5)
    mlp_w_down = nrm((DEPTH, D_FF, D_MODEL), D_FF ** -0.5)
    return {
        "x": x, "c": c, "positions": positions,
        "ada_w": ada_w, "ada_b": ada_b, "norm_pre_g": norm_pre_g, "norm_post_g": norm_post_g,
        "gla_w_in": gla_w_in, "gla_w_gate_up": gla_w_gate_up, "gla_b_gate": gla_b_gate,
        "gla_head_g": gla_head_g, "gla_w_out": gla_w_out,
        "mla_w_in": mla_w_in, "mla_q_norm_g": mla_q_norm_g, "mla_w_uq": mla_w_uq,
        "mla_kv_norm_g": mla_kv_norm_g, "mla_w_ukv": mla_w_ukv, "mla_w_out": mla_w_out,
        "gdn_w_in": gdn_w_in, "gdn_conv_w": gdn_conv_w, "gdn_a_log": gdn_a_log,
        "gdn_dt_bias": gdn_dt_bias, "gdn_norm_g": gdn_norm_g, "gdn_w_out": gdn_w_out,
        "mlp_w_up": mlp_w_up, "mlp_w_down": mlp_w_down,
    }

def reference(x, c, positions, ada_w, ada_b, norm_pre_g, norm_post_g,
              gla_w_in, gla_w_gate_up, gla_b_gate, gla_head_g, gla_w_out,
              mla_w_in, mla_q_norm_g, mla_w_uq, mla_kv_norm_g, mla_w_ukv, mla_w_out,
              gdn_w_in, gdn_conv_w, gdn_a_log, gdn_dt_bias, gdn_norm_g, gdn_w_out,
              mlp_w_up, mlp_w_down):
    cond = jax.nn.silu(c)
    for layer in range(DEPTH):
        mod = cond @ ada_w[layer] + ada_b[layer]
        sh_m, sc_m, gt_m, sh_f, sc_f, gt_f = [m[:, None, :] for m in jnp.split(mod, N_MOD, axis=-1)]

        h = rms_norm(x, norm_pre_g[layer, 0]) * (1.0 + sc_m) + sh_m
        kind, j = layer % N_MIXERS, layer // N_MIXERS
        if kind == 0:
            y = gla_mixer(h, gla_w_in[j], gla_w_gate_up[j], gla_b_gate[j], gla_head_g[j], gla_w_out[j])
        elif kind == 1:
            y = mla_mixer(h, positions, mla_w_in[j], mla_q_norm_g[j], mla_w_uq[j],
                          mla_kv_norm_g[j], mla_w_ukv[j], mla_w_out[j])
        else:
            y = gdn_mixer(h, gdn_w_in[j], gdn_conv_w[j], gdn_a_log[j], gdn_dt_bias[j],
                          gdn_norm_g[j], gdn_w_out[j])
        x = x + gt_m * rms_norm(y, norm_post_g[layer, 0])

        h = rms_norm(x, norm_pre_g[layer, 1]) * (1.0 + sc_f) + sh_f
        y = squared_relu_mlp(h, mlp_w_up[layer], mlp_w_down[layer])
        x = x + gt_f * rms_norm(y, norm_post_g[layer, 1])
    return x


_drawn_inputs = setup_inputs


def setup_inputs(seed=0):
    import zlib

    import numpy as np

    out = dict(_drawn_inputs(seed))
    spreads = {}
    factors = {'gla_b_gate': 4.079, 'mla_q_norm_g': 6.639}
    for name, (base, spread) in spreads.items():
        noise = np.random.default_rng([zlib.crc32(name.encode()), seed]).standard_normal(out[name].shape)
        drawn = base * np.exp(spread * noise) if base else spread * noise
        out[name] = jnp.asarray(drawn.astype(out[name].dtype))
    for name, factor in factors.items():
        out[name] = (out[name] * factor).astype(out[name].dtype)
    return out
```

```python
from contextlib import ExitStack

import concourse.bass as bass
from concourse import mybir

F32 = mybir.dt.float32
F32R = mybir.dt.float32r
I32 = mybir.dt.int32
ACT = mybir.ActivationFunctionType
ALU = mybir.AluOpType
AX = mybir.AxisListType.X
ds = bass.ds

P = 128
D = 1024
S = 1024
DEPTH = 2
HALF = 512
KT = D // P
CHUNK = 64
EPS = 1e-6

GLA_HEADS, GLA_DK, GLA_DV, GLA_RANK, GLA_TEMP = 4, 128, 256, 16, 16.0
NCH = S // CHUNK
MLA_HEADS, NOPE, ROPE, MLA_V, Q_RANK, KV_RANK = 16, 64, 32, 64, 384, 256
QT, KVT = Q_RANK // P, KV_RANK // P
THETA = 10000.0
D_FF = 4 * D
FB = 256
NFB = D_FF // FB

GLA_PER_HEAD = 6
U_GLR = 0
U_GLA = 1
U_GLA_OUT = U_GLA + GLA_PER_HEAD * GLA_HEADS
U_MLP0 = U_GLA_OUT + KT
MLP_UNITS = 2 * D * D_FF // (P * 1024)
U_MLA_IN = U_MLP0 + MLP_UNITS
MLA_IN_UNITS = QT + KVT + 1
U_MLA = U_MLA_IN + MLA_IN_UNITS
U_MLA_OUT = U_MLA + MLA_HEADS
U_MLP1 = U_MLA_OUT + KT
UNITS = U_MLP1 + MLP_UNITS

N_ADA = DEPTH * 6 * KT
C_PRE = N_ADA
C_POST = C_PRE + 2 * DEPTH * KT
C_BGATE = C_POST + 2 * DEPTH * KT
C_HEADG = C_BGATE + GLA_HEADS
C_QG = C_HEADG + GLA_DV // P
C_KVG = C_QG + QT
C_FREQ = C_KVG + KVT
C_SIGN = C_FREQ + 1
NCOL = C_SIGN + 1
ADA_FIRST = 2 * KT
PI = 3.1415925
TWO_PI = (6.28125, 1.9350051879882812e-03, 3.019916050561733e-07)
ROUND = 1.5 * 2.0 ** 23


class Steps:

    def __init__(self, eng, sem):
        self.eng, self.sem, self.base, self.k, self.per, self.i = eng, sem, 0, 0, 0, None

    def mark(self, ins):
        self.k += 1
        ins.then_inc(self.sem, 1)
        return self.at()

    def at(self):
        return self.base + self.k + (self.i * self.per if self.i is not None else 0)

    def link(self, ins):
        self.eng.wait_ge(self.sem, self.mark(ins))

    def enter(self, i, per):
        self.base, self.k, self.i, self.per = self.base + self.k, 0, i, per

    def leave(self, trips):
        assert self.k == self.per, f"{self.k} steps in a loop said to have {self.per}"
        self.base, self.k, self.i = self.base + self.per * trips, 0, None


def build(nc, x_in, units, ada, cols, cond_in, gate_up, pos_in, x_mid, sums_dram, out):
    ctx = ExitStack()
    AC = V = None
    with ctx:
        def sem(name):
            return ctx.enter_context(nc.semaphore(name))

        base = (nc.sbuf_base + 31) // 32 * 32
        KB = 1024

        def at(name, off, shape, dt=F32):
            return nc.alloc_sbuf_tensor_at(name, shape, dt, offset=base + off)

        X, WR, A, H, Y, T, M = 0, 32 * KB, 56 * KB, 120 * KB, 152 * KB, 184 * KB, 192 * KB
        C = 204 * KB
        x = at("x", X, [P, KT, S])
        w_raw = [at(f"w_raw{j}", WR + j * 4 * KB, [P, 1024]) for j in range(2)]
        w_hi = [at(f"w_hi{j}", WR + (8 + 4 * j) * KB, [P, 1024], F32R) for j in range(2)]
        w_lo = [at(f"w_lo{j}", WR + (16 + 4 * j) * KB, [P, 1024], F32R) for j in range(2)]
        a_hi = at("a_hi", A, [P, KT, S], F32R)
        a_lo = at("a_lo", A + 32 * KB, [P, KT, S], F32R)
        ada_first = at("ada_first", A, [P, ADA_FIRST, D])
        y = at("y", Y, [P, KT, S])
        ada_raw = [at(f"ada_raw{j}", M + j * 4 * KB, [P, D]) for j in range(2)]
        cond = at("cond", M + 8 * KB, [P, D])
        ident = at("ident", C, [P, P])
        ones = at("ones", C + 512, [P, P])
        col = at("col", C + 1024, [P, NCOL])
        mod = at("mod", C + 1792, [P, N_ADA])
        acc = at("acc", C + 2176, [P, 2])
        eps = at("eps", C + 2208, [P, 1])
        halfpi = at("halfpi", C + 2240, [P, 1])
        gla_b = at("gla_b", C + 2272, [P, 1])
        dec = at("dec", C + 2304, [P, NCH])
        mx = at("mx", C + 2368, [P, 8])
        mx2 = at("mx2", C + 2400, [P, 8])
        mx_r = at("mx_r", C + 2432, [P, 8], F32R)
        sq = [at(f"sq{j}", H + j * 2 * KB, [P, HALF]) for j in range(4)]
        nv = [at(f"nv{j}", H + (8 + 2 * j) * KB, [P, HALF]) for j in range(4)]
        nt = [at(f"nt{j}", H + (16 + 2 * j) * KB, [P, HALF]) for j in range(2)]
        rstd_y = at("rstd_y", H + 20 * KB, [P, S])
        rstd_x = at("rstd_x", H + 24 * KB, [P, S])
        hid_hi = [at(f"hid_hi{j}", H + j * 16 * KB, [P, 2, S], F32R) for j in range(2)]
        hid_lo = [at(f"hid_lo{j}", H + (8 + j * 16) * KB, [P, 2, S], F32R) for j in range(2)]
        relu = [at(f"relu{j}", T + j * 4 * KB, [P, S]) for j in range(2)]
        o_all = at("o_all", X, [P, KT, S])
        g_hi = at("g_q_hi", H, [P, S], F32R)
        g_lo = at("g_q_lo", H + 4 * KB, [P, S], F32R)
        g_k = at("g_k", H + 8 * KB, [P, S])
        g_v = at("g_v", H + 12 * KB, [P, 2, S])
        tok_hi = at("tok_hi", H + 20 * KB, [P, 8, 384], F32R)
        tok_lo = at("tok_lo", H + 32 * KB, [P, 8, 384], F32R)
        g_r = at("g_r", H + 44 * KB, [P, 2, S])
        g_t1 = at("g_t1", H + 52 * KB, [P, S])
        g_t2 = at("g_t2", H + 56 * KB, [P, S])
        glr = at("glr", H + 60 * KB, [GLA_RANK, S])
        st = [at(f"st{j}", H + (64 + j) * KB, [P, GLA_DV]) for j in range(2)]
        st_hi = [at(f"st_hi{j}", H + (66 + j) * KB, [P, GLA_DV], F32R) for j in range(2)]
        st_lo = [at(f"st_lo{j}", H + (68 + j) * KB, [P, GLA_DV], F32R) for j in range(2)]
        gate_all = at("gate_all", H + 70 * KB, [GLA_RANK, GLA_HEADS * GLA_DK])
        gate_w = at("gate_w", C + 2464, [GLA_RANK, GLA_DK])
        o_un = at("o_un", X, [P, KT, S])
        c_f = at("c_f", X, [P, QT + KVT, S])
        krope = at("krope", X + 20 * KB, [P, S])
        rstd_q = at("rstd_q", X + 24 * KB, [P, S])
        rstd_kv = at("rstd_kv", X + 28 * KB, [P, S])
        c_hi = at("c_hi", H, [P, QT + KVT, S], F32R)
        c_lo = at("c_lo", H + 20 * KB, [P, QT + KVT, S], F32R)
        p_f = [at(f"p_f{j}", H + (40 + 2 * j) * KB, [P, HALF]) for j in range(4)]
        p_hi = [at(f"p_hi{j}", H + (48 + 2 * j) * KB, [P, HALF], F32R) for j in range(4)]
        p_lo = [at(f"p_lo{j}", H + (56 + 2 * j) * KB, [P, HALF], F32R) for j in range(4)]
        sums = at("sums", T, [P, S])
        sums_all = at("sums_all", T + 4 * KB, [MLA_HEADS, S])
        k_hi = [at(f"k_hi{j}", A + (8 * j) * KB, [P, S], F32R) for j in range(2)]
        k_lo = [at(f"k_lo{j}", A + (8 * j + 4) * KB, [P, S], F32R) for j in range(2)]
        q_hi = [at(f"q_hi{j}", A + (16 + 8 * j) * KB, [P, S], F32R) for j in range(2)]
        q_lo = [at(f"q_lo{j}", A + (20 + 8 * j) * KB, [P, S], F32R) for j in range(2)]
        v_hi = [at(f"v_hi{j}", A + (32 + 8 * j) * KB, [P, 8, P], F32R) for j in range(2)]
        v_lo = [at(f"v_lo{j}", A + (36 + 8 * j) * KB, [P, 8, P], F32R) for j in range(2)]
        q_f = at("q_f", A + 48 * KB, [P, S])
        v_f = at("v_f", A + 52 * KB, [P, S])
        ident_r = at("ident_r", M, [P, P], F32R)
        rope_t = at("rope_t", M + 512, [P, HALF])
        cos_t = at("cos_t", M + 2560, [P, S])
        sin_t = at("sin_t", M + 2560 + 4 * KB, [P, S])
        ang = at("ang", H + 40 * KB, [P, S])
        turns = at("turns", H + 44 * KB, [P, S])
        pos_i = at("pos_i", H + 48 * KB, [P, S], I32)
        c_sq = [at(f"c_sq{j}", H + (52 + 2 * j) * KB, [P, HALF]) for j in range(4)]
        select = at("select", H + 40 * KB, [MLA_HEADS, S])
        recip = at("recip", H + 44 * KB, [MLA_HEADS, S])

        psum = ctx.enter_context(nc.psum_tensor("psum", [P, 8, HALF], F32))

        def ps(bank, c0=0, c1=HALF, r0=0, r1=P):
            return psum[r0:r1, bank, c0:c1]

        def pair(b, r0=0, r1=P):
            return psum[r0:r1, b:b + 2, :].rearrange("p a b -> p (a b)")

        def f(rounded):
            return rounded.bitcast(F32)

        def hs(half):
            return slice(half * HALF, (half + 1) * HALF)

        def blk(k):
            return slice(k * P, (k + 1) * P)

        def wait(eng, s, n):
            if not isinstance(n, int) or n > 0:
                eng.wait_ge(s, n)

        par_in = sem("parameters_loaded")
        cond_loaded = sem("cond_loaded")
        x_loaded = [sem(f"x_loaded{n}") for n in range(DEPTH + 1)]
        x_spilled = sem("x_spilled")
        stored = sem("out_stored")
        consts = sem("constants_made")
        w_loaded = [sem(f"w_loaded{j}") for j in range(2)]
        hi_ready = sem("w_hi_ready")
        lo_ready = sem("w_lo_ready")
        unit_done = sem("unit_done")
        ada_in = sem("ada_first_loaded")
        ada_loaded = [sem(f"ada_loaded{j}") for j in range(2)]
        ada_done = sem("ada_done")
        cond_ready = sem("cond_ready")
        act_s, dve_s = sem("act_steps"), sem("dve_steps")

        class Norm:

            def __init__(self, name):
                self.squared = sem(f"{name}_squared")
                self.summed = sem(f"{name}_summed")
                self.rstd = sem(f"{name}_rstd")

        class Pre:

            def __init__(self, name):
                self.value = sem(f"{name}_value")
                self.hi = sem(f"{name}_hi")
                self.lo = sem(f"{name}_lo")

        NX = [Norm(f"norm_x{n}") for n in range(4)]
        NY = [Norm(f"norm_y{n}") for n in range(4)]
        PRE = [Pre(f"pre{n}") for n in range(4)]
        x_new = [sem(f"x_updated{n}") for n in range(4)]
        y_zeroed = sem("y_zeroed")
        folded = sem("modulations_folded")
        ITEMS = [(half, k) for half in range(2) for k in range(KT)]

        def sub(n):
            b = n * 3 * KT
            return b, b + KT, b + 2 * KT

        def act_w(act, j, u):
            if not isinstance(u, int) or u < UNITS:
                wait(act, unit_done, u - 1)
                act.wait_ge(w_loaded[j], (u - j) * 8 + 16)
                act.activation(w_hi[j][:], w_raw[j][:], ACT.Copy).then_inc(hi_ready, 1)

        def pool_w(pool, j, u):
            if not isinstance(u, int) or u < UNITS:
                pool.wait_ge(hi_ready, u + 1)
                pool.tensor_tensor(w_lo[j][:], w_raw[j][:], f(w_hi[j][:]), ALU.subtract).then_inc(lo_ready, 1)

        def pool_units(pool, u, n):
            with pool.Fori(0, n // 2) as i:
                for d in range(2):
                    pool_w(pool, (u + d) % 2, i * 2 + (u + d + 2))

        def dve_ada(dve, V, j, a, buf):
            V.link(dve.scalar_tensor_tensor(out=buf, in0=buf, scalar=1.0, in1=cond[:], op0=ALU.mult,
                                            op1=ALU.mult, accum_out=acc[:, j:j + 1]))
            dve.tensor_tensor(mod[:, ds(a, 1)], acc[:, j:j + 1], col[:, ds(a, 1)], ALU.add).then_inc(ada_done, 1)

        def dve_ada_ring(dve, V, j, a):
            dve.wait_ge(ada_loaded[j], (a - ADA_FIRST - j) * 8 + 16)
            dve_ada(dve, V, j, a, ada_raw[j][:])

        def act_ada_load(act, j, a):
            if not isinstance(a, int) or a < N_ADA:
                if not isinstance(a, int) or a >= ADA_FIRST + 2:
                    act.wait_ge(ada_done, a - 1)
                act.dma_start(ada_raw[j][:], ada[ds(a, 1)].rearrange("a p n -> p (a n)")).then_inc(ada_loaded[j], 16)

        def act_squares(act, nm, src, items, ring):
            for n, (half, k) in enumerate(items):
                wait(act, nm.summed, n - len(ring) + 1)
                act.activation(ring[n % len(ring)][:], src[:, k, hs(half)], ACT.Square).then_inc(nm.squared, 1)

        def act_rstd(act, nm, half, bank, dst, width, seen):
            act.wait_ge(nm.summed, seen)
            AC.link(act.activation(dst[:, hs(half)], ps(bank), ACT.Ln, bias=eps[:], scale=1.0 / width))
            act.activation(dst[:, hs(half)], dst[:, hs(half)], ACT.Exp, scale=-0.5).then_inc(nm.rstd, 1)

        def pe_sums(pe, nm, items, ring, bank, first, last):
            for n, (half, k) in enumerate(items):
                pe.wait_ge(nm.squared, n + 1)
                pe.matmul(ps(bank + half), ones[:], ring[n % len(ring)][:], start=(k == first),
                          stop=(k == last)).then_inc(nm.summed, 1)

        def pe_bridge(pe, n, post, pre):
            if post:
                pe.wait_ge(*Y_DONE[n])
                pe_sums(pe, NY[n], ITEMS, sq, 4, 0, KT - 1)
            if pre:
                pe_sums(pe, NX[pre - 1], ITEMS, sq, 6, 0, KT - 1)

        def act_bridge(act, n, post, pre):
            if post:
                act.wait_ge(*Y_DONE[n])
                act_squares(act, NY[n], y, ITEMS, sq)
                for half in range(2):
                    act_rstd(act, NY[n], half, 4 + half, rstd_y, D, KT * (half + 1))
            if pre:
                m = pre - 1

                for idx, (half, k) in enumerate(ITEMS):
                    if post:
                        act.wait_ge(x_new[n], idx + 1)
                    wait(act, NX[m].summed, idx - 3)
                    act.activation(sq[idx % 4][:], x[:, k, hs(half)], ACT.Square).then_inc(NX[m].squared, 1)
                for half in range(2):
                    act_rstd(act, NX[m], half, 6 + half, rstd_x, D, KT * (half + 1))
                for idx, (half, k) in enumerate(ITEMS):
                    act.wait_ge(PRE[m].value, idx + 1)
                    act.activation(a_hi[:, k, hs(half)], nv[idx % 4][:], ACT.Copy).then_inc(PRE[m].hi, 1)

        def dve_bridge(dve, n, post, pre):
            if post:
                gate = sub(n)[2]
                if n in (0, 2):
                    dve.wait_ge(x_loaded[1 + n // 2], 16)
                for idx, (half, k) in enumerate(ITEMS):
                    if k == 0:
                        dve.wait_ge(NY[n].rstd, half + 1)
                    V.link(dve.scalar_tensor_tensor(out=nt[idx % 2][:], in0=y[:, k, hs(half)],
                                                    scalar=mod[:, gate + k:gate + k + 1],
                                                    in1=rstd_y[:, hs(half)], op0=ALU.mult, op1=ALU.mult))
                    dve.tensor_tensor(x[:, k, hs(half)], x[:, k, hs(half)], nt[idx % 2][:],
                                      ALU.add).then_inc(x_new[n], 1)
            if pre:
                m = pre - 1
                shift, scale, _ = sub(m)
                for idx, (half, k) in enumerate(ITEMS):
                    if k == 0:
                        dve.wait_ge(NX[m].rstd, half + 1)
                    wait(dve, PRE[m].lo, idx - 3)
                    V.link(dve.scalar_tensor_tensor(out=nv[idx % 4][:], in0=x[:, k, hs(half)],
                                                    scalar=mod[:, scale + k:scale + k + 1],
                                                    in1=rstd_x[:, hs(half)], op0=ALU.mult, op1=ALU.mult))
                    dve.tensor_scalar(nv[idx % 4][:], nv[idx % 4][:], mod[:, shift + k:shift + k + 1], None,
                                      ALU.add).then_inc(PRE[m].value, 1)

        def pool_pre(pool, m):
            for idx, (half, k) in enumerate(ITEMS):
                pool.wait_ge(PRE[m].hi, idx + 1)
                pool.tensor_tensor(a_lo[:, k, hs(half)], nv[idx % 4][:], f(a_hi[:, k, hs(half)]),
                                   ALU.subtract).then_inc(PRE[m].lo, 1)

        def dve_fold(dve, n, which):
            _, scale, gate = sub(n)
            if which == "scale":
                dve.scalar_tensor_tensor(out=mod[:, scale:scale + KT], in0=mod[:, scale:scale + KT], scalar=1.0,
                                         in1=col[:, C_PRE + n * KT:C_PRE + (n + 1) * KT],
                                         op0=ALU.add, op1=ALU.mult).then_inc(folded, 1)
            else:
                dve.tensor_tensor(mod[:, gate:gate + KT], mod[:, gate:gate + KT],
                                  col[:, C_POST + n * KT:C_POST + (n + 1) * KT], ALU.mult).then_inc(folded, 1)

        def pe_unit(pe, j, u, bank, between=None):
            pe.wait_ge(lo_ready, u + 1)
            n = 0
            for k in range(KT):
                for p, (w, a) in enumerate(((w_hi, a_hi), (w_hi, a_lo), (w_lo, a_hi))):
                    for half in range(2):
                        last = pe.matmul(ps(bank + half), w[j][:, blk(k)], a[:, k, hs(half)],
                                         start=(k == 0 and p == 0), stop=(k == KT - 1 and p == 2))
                        n += 1
                        if between and n % 3 == 0:
                            between(n // 3 - 1)
            last.then_inc(unit_done, 1)

        out_free = [sem(f"out_bank_free{n}") for n in range(2)]

        def pe_out(pe, n, u0):
            pe.sem_inc(out_free[n], 2)
            with pe.Fori(0, KT // 2) as i:
                for d in range(2):
                    pe.wait_ge(out_free[n], i * 2 + (d + 1))
                    pe_unit(pe, (u0 + d) % 2, i * 2 + (u0 + d), 2 * d)

        def act_out(act, n, u0, adas):
            with act.Fori(0, KT // 2) as i:
                for d in range(2):
                    j, u = (u0 + d) % 2, i * 2 + (u0 + d)
                    act_w(act, j, u + 2)
                    if adas:
                        act_ada_load(act, (ADA_OUT + d + 1) % 2, i * 2 + (ADA_OUT + d + 1))
                    act.wait_ge(unit_done, u + 1)
                    act.wait_ge(consts, 5)
                    act.activation(y[:, ds(i * 2 + d, 1), :].rearrange("p a n -> p (a n)"), pair(2 * d),
                                   ACT.Copy).then_inc(out_free[n], 1)

        ADA_OUT = ADA_FIRST + GLA_PER_HEAD * GLA_HEADS

        def dve_out_adas(dve):
            with dve.Fori(0, KT // 2) as i:
                V.enter(i, 2)
                for d in range(2):
                    dve_ada_ring(dve, V, (ADA_OUT + d) % 2, i * 2 + (ADA_OUT + d))
                V.leave(KT // 2)

        relu_ready = [sem(f"relu_ready{n}") for n in range(2)]
        up_value = [sem(f"up_value{n}") for n in range(2)]
        up_hi = [sem(f"up_hi{n}") for n in range(2)]
        up_lo = [sem(f"up_lo{n}") for n in range(2)]
        down_sum = [sem(f"down_sum{n}") for n in range(2)]
        down_free = [sem(f"down_free{n}") for n in range(2)]

        def mlp_plan(run, loop):
            run("up", 0, 0, 0, None)
            with loop(0, NFB // 2 - 1) as i:
                run("up", 1, 1, 2, i)
                run("down", 0, 0, 4, i)
                run("up", 2, 0, 6, i)
                run("down", 1, 1, 8, i)
            e = 2 + 4 * (NFB - 2)
            run("up", NFB - 1, 1, e, None)
            run("down", NFB - 2, 0, e + 2, None)
            run("down", NFB - 1, 1, e + 4, None)

        def plus(i, step, c):
            return c if i is None else i * step + c

        def pe_mlp(pe, m, u0):
            def run(kind, b, par, n, i):
                for d in range(2):
                    j, u = (u0 + n + d) % 2, plus(i, 8, u0 + n + d)
                    if kind == "up":
                        wait(pe, up_value[m], plus(i, 4, 2 * b + d - 1))
                        pe_unit(pe, j, u, 2 * d)
                        continue
                    pe.wait_ge(lo_ready, u + 1)
                    pe.wait_ge(up_lo[m], plus(i, 4, 2 * b + 2))
                    for q in range(4):
                        bank = 4 + 2 * (q % 2)
                        wait(pe, down_free[m], plus(i, 16, 8 * b + 4 * d + q + 1))
                        for k in range(2):
                            for p, (w, a) in enumerate(((w_hi, hid_hi), (w_hi, hid_lo), (w_lo, hid_hi))):
                                for half in range(2):
                                    last = pe.matmul(ps(bank + half), w[j][:, blk(2 * q + k)],
                                                     a[par][:, k, hs(half)], start=(k == 0 and p == 0),
                                                     stop=(k == 1 and p == 2))
                        if q < 3:
                            last.then_inc(down_sum[m], 1)
                    last.then_inc(unit_done, 1)
            pe.sem_inc(down_free[m], 2)
            mlp_plan(run, pe.Fori)

        def act_mlp(act, m, u0, adas):
            def run(kind, b, par, n, i):
                for d in range(2):
                    j, u = (u0 + n + d) % 2, plus(i, 8, u0 + n + d)
                    if adas and (kind, b, par) in ADA_AT:
                        a0 = ADA_AT[kind, b, par]
                        if a0 is not None and d < a0[1]:
                            act_ada_load(act, (a0[0] + d + 1) % 2, plus(i, 6, a0[0] + d + 1))
                    act_w(act, j, u + 2)
                    if kind == "up":
                        act.wait_ge(unit_done, u + 1)
                        wait(act, up_lo[m], plus(i, 4, 2 * b + d - 1))
                        act.activation(relu[d][:], pair(2 * d), ACT.Relu).then_inc(relu_ready[m], 1)
                        act.wait_ge(up_value[m], plus(i, 4, 2 * b + d + 1))
                        act.activation(hid_hi[par][:, d, :], relu[d][:], ACT.Copy).then_inc(up_hi[m], 1)
            mlp_plan(run, act.Fori)

        def dve_mlp(dve, m, u0, adas):
            def run(kind, b, par, n, i):
                if i is not None and (b, kind) == (1, "up"):
                    V.enter(i, 6 if adas else 0)
                for d in range(2):
                    u = plus(i, 8, u0 + n + d)
                    if adas and ADA_AT.get((kind, b, par)) and d < ADA_AT[kind, b, par][1]:
                        a0 = ADA_AT[kind, b, par][0]
                        dve_ada_ring(dve, V, (a0 + d) % 2, plus(i, 6, a0 + d))
                    if kind == "up":
                        dve.wait_ge(relu_ready[m], plus(i, 4, 2 * b + d + 1))
                        dve.scalar_tensor_tensor(out=relu[d][:], in0=pair(2 * d), scalar=0.0, in1=relu[d][:],
                                                 op0=ALU.max, op1=ALU.mult).then_inc(up_value[m], 1)
                        dve.wait_ge(up_hi[m], plus(i, 4, 2 * b + d + 1))
                        dve.tensor_tensor(hid_lo[par][:, d, :], relu[d][:], f(hid_hi[par][:, d, :]),
                                          ALU.subtract).then_inc(up_lo[m], 1)
                        continue
                    for q in range(4):
                        if q < 3:
                            dve.wait_ge(down_sum[m], plus(i, 12, 6 * b + 3 * d + q + 1))
                        else:
                            dve.wait_ge(unit_done, u + 1)
                        t = 4 * d + q
                        dve.tensor_tensor(y[:, t, :], y[:, t, :], pair(4 + 2 * (q % 2)), ALU.add).then_inc(down_free[m], 1)
                if i is not None and (b, kind) == (1, "down"):
                    V.leave(NFB // 2 - 1)
            dve.wait_ge(y_zeroed, m + 1)
            mlp_plan(run, dve.Fori)

        A1 = 6 * KT
        ADA_AT = {("up", 0, 0): (A1, 2), ("up", 1, 1): (A1 + 2, 2), ("down", 0, 0): (A1 + 4, 2),
                  ("up", 2, 0): (A1 + 6, 2), ("up", NFB - 1, 1): (A1 + 44, 2), ("down", NFB - 2, 0): (A1 + 46, 2)}

        gw_ready, gate_sum, gate_ln, gate_cum, decay_ready, kend = (sem(f"gla_{s}") for s in (
            "gate_weights", "gate_sum", "gate_ln", "gate_cum", "decay", "k_end"))
        a_ev, q_hi_s, q_lo_s = sem("gla_evacuated"), sem("gla_q_hi"), sem("gla_q_lo")
        tok_sum, tok_hi_s, tok_lo_s = sem("gla_transposed"), sem("gla_tok_hi"), sem("gla_tok_lo")
        kv_sum, st_new, st_hi_s, st_lo_s, o_sum, o_ev = (sem(f"gla_{s}") for s in (
            "kv_sum", "state", "state_hi", "state_lo", "o_sum", "o_evacuated"))
        o_normed, o_hi_s, o_lo_s = sem("gla_o_normed"), sem("gla_o_hi"), sem("gla_o_lo")
        NG = Norm("gla_head")
        QSCALE = GLA_DK ** -0.5

        def pe_gla(pe):
            pe_unit(pe, U_GLR % 2, U_GLR, 4)
            with pe.Fori(0, GLA_HEADS) as i:
                def u(d):
                    return (U_GLA + d) % 2, i * GLA_PER_HEAD + (U_GLA + d)
                pe.wait_ge(gw_ready, i + 1)
                pe.wait_ge(a_ev, i * 4 + 1)
                pe.wait_ge(NG.rstd, i * 2 + 2)
                for half in range(2):
                    last = pe.matmul(ps(4 + half), gate_w[:], glr[:, hs(half)], start=True, stop=True)
                last.then_inc(gate_sum, 1)
                pe_unit(pe, *u(0), 0)
                pe_unit(pe, *u(1), 2)
                pe.wait_ge(kend, i + 1)
                pe_unit(pe, *u(2), 0)
                pe.wait_ge(a_ev, i * 4 + 2)
                pe_unit(pe, *u(3), 2)
                pe.wait_ge(a_ev, i * 4 + 3)
                pe.wait_ge(o_ev, i * 4 + 4)
                for t in range(8):
                    if t >= 2:
                        pe.wait_ge(tok_lo_s, i * 8 + (t - 1))
                    for c, src in enumerate((g_k[:, blk(t)], g_v[:, 0, blk(t)], g_v[:, 1, blk(t)])):
                        last = pe.transpose(ps(6 + t % 2, c * P, c * P + P), src, ident[:])
                    last.then_inc(tok_sum, 1)
                pe_unit(pe, *u(4), 0)

                def kv(n):
                    t, r = n // 2, slice(64 * (n % 2), 64 * (n % 2) + 64)
                    if n >= 2:
                        pe.wait_ge(st_new, i * NCH + (n - 1))
                    for p, (k_, v_) in enumerate(((tok_hi, tok_hi), (tok_hi, tok_lo), (tok_lo, tok_hi))):
                        last = pe.matmul(ps(4 + n % 2, 0, GLA_DV), k_[r, t, 0:P], v_[r, t, P:384],
                                         start=(p == 0), stop=(p == 2))
                    last.then_inc(kv_sum, 1)

                def read(m):
                    pe.wait_ge(st_lo_s, i * NCH + (m + 1))
                    if m % 4 == 0 and m >= 8:
                        pe.wait_ge(o_ev, i * 4 + (m // 4 + 3))
                    cs = slice(m * CHUNK, (m + 1) * CHUNK)
                    for dt in range(2):
                        c0 = dt * 256 + (m % 4) * CHUNK
                        for p, (s_, q_) in enumerate(((st_hi, g_hi), (st_hi, g_lo), (st_lo, g_hi))):
                            last = pe.matmul(ps(6 + (m // 4) % 2, c0, c0 + CHUNK), s_[m % 2][:, blk(dt)],
                                             q_[:, cs], start=(p == 0), stop=(p == 2))
                    last.then_inc(o_sum, 1)

                def scan(n):
                    kv(n)
                    if n:
                        read(n - 1)
                pe.wait_ge(q_lo_s, i + 1)
                pe.wait_ge(tok_lo_s, i * 8 + 8)
                pe_unit(pe, *u(5), 2, between=scan)
                read(NCH - 1)
                for half in range(2):
                    pe.wait_ge(NG.squared, i * 4 + (half * 2 + 2))
                    for dt in range(2):
                        last = pe.matmul(ps(4 + half), ones[:], g_v[:, dt, hs(half)], start=(dt == 0), stop=(dt == 1))
                    last.then_inc(NG.summed, 1)
            pe.wait_ge(o_lo_s, KT)

        def act_gla(act):
            act_w(act, U_GLR % 2, U_GLR + 2)
            act.wait_ge(unit_done, U_GLR + 1)
            act.activation(glr[:], pair(4, 0, GLA_RANK), ACT.Copy).then_inc(a_ev, 1)
            act.sem_inc(NG.rstd, 2)
            act.sem_inc(o_ev, 4)
            with act.Fori(0, GLA_HEADS) as i:
                AC.enter(i, 2 + 2)

                def unit(d):
                    act_w(act, (U_GLA + d) % 2, i * GLA_PER_HEAD + (U_GLA + d + 2))
                    act_ada_load(act, (ADA_FIRST + d + 1) % 2, i * GLA_PER_HEAD + (ADA_FIRST + d + 1))
                    act.wait_ge(unit_done, i * GLA_PER_HEAD + (U_GLA + d + 1))
                act.wait_ge(gate_sum, i + 1)
                AC.link(act.activation(g_t1[:], pair(4), ACT.Abs, bias=gla_b[:]))
                AC.link(act.activation(g_t1[:], g_t1[:], ACT.Exp, scale=-1.0))
                act.activation(g_t1[:], g_t1[:], ACT.Ln, bias=ones[:, 0:1]).then_inc(gate_ln, 1)
                act.wait_ge(gate_cum, i + 1)
                act.activation(g_t2[:], g_t2[:], ACT.Exp, scale=1.0 / GLA_TEMP).then_inc(decay_ready, 1)
                act.activation(dec[:], g_t1[:].rearrange("p (n l) -> p n l", l=CHUNK)[:, :, CHUNK - 1],
                               ACT.Exp, scale=1.0 / GLA_TEMP).then_inc(decay_ready, 1)
                unit(0)
                for dt in range(2):
                    unit(1 + dt)
                    act.activation(g_v[:, dt, :], pair(2 - 2 * dt), ACT.Copy).then_inc(a_ev, 1)
                unit(3)
                act.activation(g_hi[:], pair(2), ACT.Copy, scale=QSCALE).then_inc(q_hi_s, 1)
                for t in range(8):
                    act.wait_ge(tok_sum, i * 8 + (t + 1))
                    act.activation(tok_hi[:, t, :], ps(6 + t % 2, 0, 384), ACT.Copy).then_inc(tok_hi_s, 1)
                unit(4)
                act.activation(g_r[:, 0, :], pair(0), ACT.Silu).then_inc(a_ev, 1)

                def leave(g):
                    act.wait_ge(o_sum, i * NCH + (4 * g + 4))
                    act.activation(g_v[:, :, 256 * g:256 * g + 256], ps(6 + g % 2).rearrange("p (a l) -> p a l", a=2),
                                   ACT.Square).then_inc(NG.squared, 1)
                    act.activation(o_all[:, ds(i * 2, 2), 256 * g:256 * g + 256],
                                   ps(6 + g % 2).rearrange("p (a l) -> p a l", a=2), ACT.Copy).then_inc(o_ev, 1)
                for n in range(NCH):
                    act.wait_ge(st_new, i * NCH + (n + 1))
                    if n >= 2:
                        act.wait_ge(o_sum, i * NCH + (n - 1))
                    act.activation(st_hi[n % 2][:], st[n % 2][:], ACT.Copy).then_inc(st_hi_s, 1)
                    if n % 4 == 1 and n > 4:
                        leave(n // 4 - 1)
                leave(3)
                unit(5)
                act.activation(g_r[:, 1, :], pair(2), ACT.Silu).then_inc(a_ev, 1)
                for half in range(2):
                    act.wait_ge(NG.summed, i * 2 + (half + 1))
                    AC.link(act.activation(g_t2[:, hs(half)], ps(4 + half), ACT.Ln, bias=eps[:], scale=1.0 / GLA_DV))
                    act.activation(g_t2[:, hs(half)], g_t2[:, hs(half)], ACT.Exp, scale=-0.5).then_inc(NG.rstd, 1)
                AC.leave(GLA_HEADS)
            for k in range(KT):
                act.wait_ge(o_normed, 4 * (k // 2 + 1))
                act.activation(a_hi[:, k, :], o_all[:, k, :], ACT.Copy).then_inc(o_hi_s, 1)
            act.wait_ge(o_lo_s, KT)
            act.dma_start(x[:], x_in).then_inc(x_loaded[1], 16)

        def dve_gla(dve):
            with dve.Fori(0, GLA_HEADS) as i:
                V.enter(i, 1 + 1 + NCH + 1 + 4 + GLA_PER_HEAD)

                def ada_col(d):
                    dve_ada_ring(dve, V, (ADA_FIRST + d) % 2, i * GLA_PER_HEAD + (ADA_FIRST + d))
                dve.tensor_copy(gate_w[:], gate_all[:, ds(i * GLA_DK, GLA_DK)])
                dve.tensor_copy(gla_b[:], col[:, ds(i + C_BGATE, 1)]).then_inc(gw_ready, 1)
                dve.wait_ge(gw_ready, i + 1)
                dve.wait_ge(gate_ln, i + 1)
                V.link(dve.tensor_scalar(g_t2[:], pair(4), gla_b[:], 0.0, ALU.add, ALU.min))
                V.link(dve.tensor_tensor(g_t2[:], g_t2[:], g_t1[:], ALU.subtract))
                for n in range(NCH):
                    cs = slice(n * CHUNK, (n + 1) * CHUNK)
                    last = V.mark(dve.tensor_tensor_scan(out=g_t1[:, cs], data0=ones[:, 0:CHUNK], data1=g_t2[:, cs],
                                                         initial=0.0, op0=ALU.mult, op1=ALU.add))
                dve.wait_ge(dve_s, last)
                cum = g_t1[:].rearrange("p (n l) -> p n l", l=CHUNK)
                dve.tensor_tensor(g_t2[:].rearrange("p (n l) -> p n l", l=CHUNK),
                                  cum[:, :, CHUNK - 1:CHUNK].to_broadcast([P, NCH, CHUNK]), cum,
                                  ALU.subtract).then_inc(gate_cum, 1)
                ada_col(0)
                dve.wait_ge(unit_done, i * GLA_PER_HEAD + (U_GLA + 1))
                dve.wait_ge(decay_ready, i * 2 + 1)
                dve.tensor_tensor(g_k[:], pair(0), g_t2[:], ALU.mult).then_inc(kend, 1)
                for d in range(1, 4):
                    ada_col(d)
                dve.wait_ge(q_hi_s, i + 1)
                dve.scalar_tensor_tensor(out=g_lo[:], in0=pair(2), scalar=QSCALE, in1=f(g_hi[:]), op0=ALU.mult,
                                         op1=ALU.subtract).then_inc(q_lo_s, 1)
                for t in range(8):
                    dve.wait_ge(tok_hi_s, i * 8 + (t + 1))
                    dve.tensor_tensor(tok_lo[:, t, :], ps(6 + t % 2, 0, 384), f(tok_hi[:, t, :]),
                                      ALU.subtract).then_inc(tok_lo_s, 1)
                ada_col(4)
                V.link(dve.memset(st[1][:], 0.0))

                def state(n):
                    dve.wait_ge(kv_sum, i * NCH + (n + 1))
                    if n == 0:
                        dve.wait_ge(decay_ready, i * 2 + 2)
                    else:
                        dve.wait_ge(st_new, i * NCH + n)
                    dve.scalar_tensor_tensor(out=st[n % 2][:], in0=st[(n + 1) % 2][:], scalar=dec[:, n:n + 1],
                                             in1=ps(4 + n % 2, 0, GLA_DV), op0=ALU.mult,
                                             op1=ALU.add).then_inc(st_new, 1)
                state(0)
                for n in range(NCH):
                    dve.wait_ge(st_hi_s, i * NCH + (n + 1))
                    if n >= 2:
                        dve.wait_ge(o_sum, i * NCH + (n - 1))
                    dve.tensor_tensor(st_lo[n % 2][:], st[n % 2][:], f(st_hi[n % 2][:]), ALU.subtract).then_inc(st_lo_s, 1)
                    if n + 1 < NCH:
                        state(n + 1)
                ada_col(5)
                dve.wait_ge(a_ev, i * 4 + 5)
                for half in range(2):
                    dve.wait_ge(NG.rstd, i * 2 + (half + 3))
                    for dt in range(2):
                        o = o_all[:, ds(i * 2 + dt, 1), hs(half)].rearrange("p a n -> p (a n)")
                        V.link(dve.scalar_tensor_tensor(out=o, in0=o, scalar=col[:, C_HEADG + dt:C_HEADG + dt + 1],
                                                        in1=g_t2[:, hs(half)], op0=ALU.mult, op1=ALU.mult))
                        dve.tensor_tensor(o, o, g_r[:, dt, hs(half)], ALU.mult).then_inc(o_normed, 1)
                V.leave(GLA_HEADS)
            for k in range(KT):
                dve.wait_ge(o_hi_s, k + 1)
                dve.tensor_tensor(a_lo[:, k, :], o_all[:, k, :], f(a_hi[:, k, :]), ALU.subtract).then_inc(o_lo_s, 1)

        NQ, NKV = Norm("mla_q"), Norm("mla_kv")
        ang_s, sin_s, tables = sem("rope_angles"), sem("rope_sines"), sem("rope_tables")
        pos_loaded, ident_s = sem("positions_loaded"), sem("identity_rounded")
        c_ev, kr_s, c_val, c_hi_s, c_lo_s = (sem(f"mla_{s}") for s in ("c_evacuated", "k_rope", "c_value", "c_hi", "c_lo"))
        fixed_s, pad_s = sem("mla_shared_rows"), sem("mla_pads")
        sc_sum, p_exp, p_hi_s, p_lo_s, pv_done = (sem(f"mla_{s}") for s in (
            "scores", "p_exp", "p_hi", "p_lo", "pv_done"))
        prep, qf_s, rp_s, qhi_s, qlo_s, khi_s, klo_s, vf_s = (sem(f"mla_{s}") for s in (
            "projected", "q_copied", "q_roped", "q_hi", "q_lo", "k_hi", "k_lo", "v_copied"))
        vt_sum, vhi_s, vlo_s, mx_sum, mx_used, mx_s, row_sum, row_s = (sem(f"mla_{s}") for s in (
            "v_transposed", "v_hi", "v_lo", "max_scores", "max_read", "max", "max_rows", "max_row_set"))
        sums_back = sem("mla_sums_back")
        o_out, sums_kept = sem("mla_o_evacuated"), [sem(f"mla_sums_kept{j}") for j in range(2)]
        sel_s, rec_s, bc_sum, on_s, oh_s, ol_s = (sem(f"mla_{s}") for s in (
            "selector", "reciprocals", "reciprocals_spread", "o_normed", "o_hi", "o_lo"))
        SM = (NOPE + ROPE) ** -0.5
        R0, R1, R2 = NOPE, NOPE + ROPE, NOPE + 2 * ROPE
        DT = NOPE + ROPE
        QI = [(half, k) for half in range(2) for k in range(QT)]
        KI = [(half, k) for half in range(2) for k in range(QT, QT + KVT)]
        BLOCKS = [(half, j, max(P * j, HALF * half), HALF * (half + 1)) for half in range(2) for j in range(4 * half + 4)]
        NB = len(BLOCKS)

        def pe_mla_in(pe):
            for m in range(MLA_IN_UNITS):
                u = U_MLA_IN + m
                wait(pe, c_ev, m - 1)
                pe_unit(pe, u % 2, u, 2 * (m % 2))
            pe_sums(pe, NQ, QI, c_sq, 4, 0, QT - 1)
            pe_sums(pe, NKV, KI, c_sq, 6, QT, QT + KVT - 1)

        def act_mla_in(act):
            act.wait_ge(PRE[2].lo, 2 * KT)
            act.dma_start(x_mid, x[:]).then_inc(x_spilled, 16)
            act.dma_start(pos_i[R0:R1], pos_in).then_inc(pos_loaded, 16)
            act.wait_ge(ada_done, N_ADA)
            act.activation(ident_r[:], ident[:], ACT.Copy).then_inc(ident_s, 1)
            act.wait_ge(ang_s, 1)
            act.activation(sin_t[R0:R1], ang[R0:R1], ACT.Sin).then_inc(sin_s, 1)
            AC.link(act.activation(turns[R0:R1], ang[R0:R1], ACT.Abs))
            act.activation(cos_t[R0:R1], turns[R0:R1], ACT.Sin, bias=halfpi[R0:R1], scale=-1.0).then_inc(sin_s, 1)
            act.wait_ge(x_spilled, 16)
            for m in range(MLA_IN_UNITS):
                u = U_MLA_IN + m
                act_w(act, u % 2, u + 2)
                act.wait_ge(unit_done, u + 1)
                if m < MLA_IN_UNITS - 1:
                    act.activation(c_f[:, m, :], pair(2 * (m % 2)), ACT.Copy).then_inc(c_ev, 1)
            act.wait_ge(c_ev, MLA_IN_UNITS - 1)
            act_squares(act, NQ, c_f, QI, c_sq)
            act.wait_ge(NQ.summed, len(QI))
            act_squares(act, NKV, c_f, KI, c_sq)
            for half in range(2):
                act_rstd(act, NQ, half, 4 + half, rstd_q, Q_RANK, QT * (half + 1))
            for half in range(2):
                act_rstd(act, NKV, half, 6 + half, rstd_kv, KV_RANK, KVT * (half + 1))
            for m in range(QT + KVT):
                act.wait_ge(c_val, m + 1)
                act.activation(c_hi[:, m, :], c_f[:, m, :], ACT.Copy).then_inc(c_hi_s, 1)
            act.wait_ge(kr_s, 1)
            for j in range(2):
                act.activation(k_hi[j][R0:R1], krope[R0:R1], ACT.Copy).then_inc(fixed_s, 1)

        def dve_mla_in(dve):
            dve.wait_ge(pos_loaded, 16)
            F, G = slice(R0, R1), col[R0:R1, C_FREQ:C_FREQ + 1]
            V.link(dve.tensor_copy(ang[F], pos_i[F]))
            V.link(dve.tensor_scalar(ang[F], ang[F], G, None, ALU.mult))
            V.link(dve.tensor_scalar(turns[F], ang[F], 0.15915494309189535, ROUND, ALU.mult, ALU.add))
            V.link(dve.tensor_scalar(turns[F], turns[F], ROUND, None, ALU.subtract))
            for c in TWO_PI:
                V.link(dve.scalar_tensor_tensor(out=ang[F], in0=turns[F], scalar=-c, in1=ang[F], op0=ALU.mult, op1=ALU.add))
            dve.tensor_scalar(ang[F], ang[F], PI, -PI, ALU.min, ALU.max).then_inc(ang_s, 1)
            dve.wait_ge(sin_s, 2)
            dve.tensor_scalar(sin_t[F], sin_t[F], col[F, C_SIGN:C_SIGN + 1], None, ALU.mult).then_inc(tables, 1)
            dve.wait_ge(tables, 1)
            dve.wait_ge(x_spilled, 16)
            dve.wait_ge(unit_done, U_MLA_IN + MLA_IN_UNITS)
            b = 2 * ((MLA_IN_UNITS - 1) % 2)
            V.link(dve.tensor_tensor(krope[F], pair(b, R0, R1), cos_t[F], ALU.mult))
            for half in range(2):
                V.link(dve.tensor_tensor(rope_t[F], ps(b + half, r0=R1, r1=R2), sin_t[F, hs(half)], ALU.mult))
                last = V.mark(dve.tensor_tensor(krope[F, hs(half)], krope[F, hs(half)], rope_t[F], ALU.add))
                dve.wait_ge(dve_s, last)
            dve.sem_inc(kr_s, 1)
            for m in range(QT + KVT):
                r = (rstd_q if m < QT else rstd_kv)
                dve.wait_ge(NQ.rstd if m < QT else NKV.rstd, 2)
                dve.scalar_tensor_tensor(out=c_f[:, m, :], in0=c_f[:, m, :], scalar=col[:, C_QG + m:C_QG + m + 1],
                                         in1=r[:], op0=ALU.mult, op1=ALU.mult).then_inc(c_val, 1)
            for m in range(QT + KVT):
                dve.wait_ge(c_hi_s, m + 1)
                dve.tensor_tensor(c_lo[:, m, :], c_f[:, m, :], f(c_hi[:, m, :]), ALU.subtract).then_inc(c_lo_s, 1)
            for j in range(2):
                dve.wait_ge(fixed_s, j + 1)
                dve.tensor_tensor(k_lo[j][F], krope[F], f(k_hi[j][F]), ALU.subtract).then_inc(kr_s, 1)

        def pool_pads(pool):
            pool.wait_ge(unit_done, U_MLA_IN + MLA_IN_UNITS)
            pool.wait_ge(lo_ready, U_MLA + 2)
            n = 0
            for j in range(2):
                c = MLA_V * (1 - j)
                for t, v in ((k_hi[j][DT:DT + 1], -1.0), (k_lo[j][DT:DT + 1], 0.0), (q_lo[j][DT:DT + 1], 0.0),
                             (v_lo[j][:, :, c:c + 64], 0.0), (v_hi[j][:, :, c + 1:c + 64], 0.0),
                             (v_hi[j][:, :, c:c + 1], 1.0)):
                    wait(pool, pad_s, n)
                    pool.memset(f(t), v).then_inc(pad_s, 1)
                    n += 1
            pool.wait_ge(pad_s, n)

        def pe_prep(pe, s, h, j, i):
            def c(k, d=0):
                return plus(i, 2 * k, k * h + d)
            if s < 4:
                kind, half = s // 2, s % 2
                if s == 0:
                    pe.wait_ge(lo_ready, plus(i, 2, U_MLA + h + 1))
                if kind == 0:
                    wait(pe, mx_used, c(8))
                else:
                    wait(pe, row_s, c(1))
                tiles = range(QT) if kind == 0 else range(QT, QT + KVT)
                for t in tiles:
                    for p, (w, a) in enumerate(((w_hi, c_hi), (w_hi, c_lo), (w_lo, c_hi))):
                        last = pe.matmul(ps(4 + s), w[(U_MLA + j) % 2][:, blk(t)], a[:, t, hs(half)],
                                         start=(t == tiles[0] and p == 0), stop=(t == tiles[-1] and p == 2))
                last.then_inc(prep if s < 3 else unit_done, 1)
            elif s == 5:
                for t in range(8):
                    last = pe.transpose(ps(4, 64 * t, 64 * t + 64), v_f[64:128, blk(t)], ident[64:128, 64:128])
                last.then_inc(vt_sum, 1)
            elif 6 <= s < 10:
                if s == 6:
                    pe.wait_ge(qhi_s, c(2, 2))
                    pe.wait_ge(klo_s, c(2, 2))
                    pe.wait_ge(fixed_s, 2)
                for t in (2 * (s - 6), 2 * (s - 6) + 1):
                    if t == 1:
                        pe.wait_ge(vlo_s, c(1, 1))
                    if t >= 2:
                        pe.wait_ge(mx_used, c(8, t - 1))
                    b = 6 - 2 * (t % 2)
                    for k0 in range(0, P * (t + 1), HALF):
                        k1 = min(k0 + HALF, P * (t + 1))
                        last = pe.matmul(ps(b + k0 // HALF, 0, k1 - k0), q_hi[j][0:R1, blk(t)], k_hi[j][0:R1, k0:k1],
                                         start=True, stop=True)
                    last.then_inc(mx_sum, 1)
            elif s == 12:
                pe.wait_ge(mx_s, c(1, 1))
                for t in range(8):
                    last = pe.matmul(ps(6 + t // 4, P * (t % 4), P * (t % 4) + P),
                                     mx_r[:, t:t + 1].to_broadcast([P, P]), ident_r[:], start=True, stop=True)
                last.then_inc(row_sum, 1)

        def projected(eng, s, h, i):
            if s < 3:
                eng.wait_ge(prep, plus(i, 6, 3 * h + s + 1))
            else:
                eng.wait_ge(unit_done, plus(i, 2, U_MLA + h + 1))

        def act_prep(act, s, h, j, i):
            def c(k, d=0):
                return plus(i, 2 * k, k * h + d)
            if s < 4:
                kind, half = s // 2, s % 2
                projected(act, s, h, i)
                if kind == 0:
                    wait(act, qlo_s, c(2, half - 1))
                    act.activation(q_f[0:R0, hs(half)], ps(4 + s, r1=R0), ACT.Copy).then_inc(qf_s, 1)
                else:
                    act.activation(k_hi[j][0:R0, hs(half)], ps(4 + s, r1=R0), ACT.Copy).then_inc(khi_s, 1)
                    act.activation(v_f[R0:P, hs(half)], ps(4 + s, r0=R0), ACT.Copy).then_inc(vf_s, 1)
            elif s == 4:
                for half in range(2):
                    act.wait_ge(rp_s, c(2, half + 1))
                    act.wait_ge(qf_s, c(2, half + 1))
                    act.activation(q_hi[j][0:R1, hs(half)], q_f[0:R1, hs(half)], ACT.Copy).then_inc(qhi_s, 1)
                act_w(act, (U_MLA + j) % 2, plus(i, 2, U_MLA + h + 2))
            elif s == 5:
                act.wait_ge(vt_sum, c(1, 1))
                act.activation(v_hi[j][:, :, 64 * j:64 * j + 64], ps(4).rearrange("p (t c) -> p t c", c=64),
                               ACT.Copy).then_inc(vhi_s, 1)
            elif s == 12:
                act.wait_ge(row_sum, c(1, 1))
                act.activation(q_hi[j][DT:DT + 1], pair(6, DT, DT + 1), ACT.Copy).then_inc(row_s, 1)

        def dve_prep(dve, s, h, j, i):
            def c(k, d=0):
                return plus(i, 2 * k, k * h + d)
            if s < 2:
                projected(dve, s, h, i)
                V.link(dve.tensor_tensor(q_f[R0:R1, hs(s)], ps(4 + s, r0=R0, r1=R1), cos_t[R0:R1, hs(s)], ALU.mult))
                V.link(dve.tensor_tensor(rope_t[R0:R1], ps(4 + s, r0=R1, r1=R2), sin_t[R0:R1, hs(s)], ALU.mult))
                dve.tensor_tensor(q_f[R0:R1, hs(s)], q_f[R0:R1, hs(s)], rope_t[R0:R1], ALU.add).then_inc(rp_s, 1)
                dve.wait_ge(rp_s, c(2, s + 1))
            elif s < 4:
                half = s % 2
                dve.wait_ge(khi_s, c(2, half + 1))
                dve.tensor_tensor(k_lo[j][0:R0, hs(half)], ps(4 + s, r1=R0), f(k_hi[j][0:R0, hs(half)]),
                                  ALU.subtract).then_inc(klo_s, 1)
            elif s == 4:
                for half in range(2):
                    dve.wait_ge(qhi_s, c(2, half + 1))
                    dve.tensor_tensor(q_lo[j][0:R1, hs(half)], q_f[0:R1, hs(half)], f(q_hi[j][0:R1, hs(half)]),
                                      ALU.subtract).then_inc(qlo_s, 1)
            elif s == 5:
                dve.wait_ge(vhi_s, c(1, 1))
                vs = slice(64 * j, 64 * j + 64)
                dve.tensor_tensor(v_lo[j][:, :, vs], ps(4).rearrange("p (t c) -> p t c", c=64), f(v_hi[j][:, :, vs]),
                                  ALU.subtract).then_inc(vlo_s, 1)
            elif 6 <= s < 10:
                for t in (2 * (s - 6), 2 * (s - 6) + 1):
                    dve.wait_ge(mx_sum, c(8, t + 1))
                    src = psum[:, 6 - 2 * (t % 2):8 - 2 * (t % 2), :].rearrange("p a b -> p (a b)")
                    n = P * t + CHUNK
                    V.mark(dve.reduce_max(mx[:, t:t + 1], src[:, 0:n], axis=AX))
                    dve.reduce_max(mx2[64:128, t:t + 1], src[64:128, n:n + CHUNK], axis=AX).then_inc(mx_used, 1)
                if s == 9:
                    dve.wait_ge(mx_used, c(8, 8))
                    dve.wait_ge(dve_s, V.at())
                    V.link(dve.tensor_tensor(mx[64:128], mx[64:128], mx2[64:128], ALU.max))
                    wait(dve, row_s, c(1))
                    dve.tensor_copy(mx_r[:], mx[:]).then_inc(mx_s, 1)

        PREP_V = 2 * 2 + 8 + 1

        def pe_v_ready(pe, h, i):
            for s_ in (vf_s, qf_s, rp_s):
                pe.wait_ge(s_, plus(i, 4, 2 * h + 2))

        def pe_head(pe, h, j, i, follow):
            def c(k, d=0):
                return plus(i, 2 * k, k * h + d)
            pe.wait_ge(row_s, c(1, 1))
            pe.wait_ge(qlo_s, c(2, 2))
            if h == 0 and i is not None:
                pe.wait_ge(pad_s, 12)
                pe.wait_ge(kr_s, 3)
            for s in range(NB + 3):
                if follow and s == 5:
                    pe_v_ready(pe, h + 1, i)
                if s < NB:
                    half, t, q0, q1 = BLOCKS[s]
                    pe.wait_ge(p_exp, c(NB, s + 1))
                    for p, (k_, q_) in enumerate(((k_hi, q_hi), (k_hi, q_lo), (k_lo, q_hi))):
                        last = pe.matmul(ps(2 + s % 2, 0, q1 - q0), k_[j][0:DT + 1, blk(t)], q_[j][0:DT + 1, q0:q1],
                                         start=(p == 0), stop=(p == 2))
                    last.then_inc(sc_sum, 1)
                if follow:
                    pe_prep(pe, s, h + 1, 1 - j, i)
                if s >= 3:
                    m = s - 3
                    half, t, q0, q1 = BLOCKS[m]
                    pe.wait_ge(p_lo_s, c(NB, m + 5))
                    if t == 0:
                        pe.wait_ge(o_out, c(2, half + 1))
                    b0 = q0 - HALF * half
                    for p, (v_, p_) in enumerate(((v_hi, p_hi), (v_hi, p_lo), (v_lo, p_hi))):
                        last = pe.matmul(ps(half, b0, HALF), v_[j][:, t, :], p_[m % 4][:, 0:q1 - q0],
                                         start=(t == 0 and p == 0), stop=(t == 4 * half + 3 and p == 2))
                    last.then_inc(pv_done, 1)

        def act_head(act, h, j, i, follow):
            def c(k, d=0):
                return plus(i, 2 * k, k * h + d)
            rows = slice(64 * j, 64 * j + 64)
            srow = 64 * (1 - j)

            def leave(half):
                act.wait_ge(pv_done, c(NB, (4 if half == 0 else NB) + 4))
                act.wait_ge(consts, 5)
                act.activation(o_un[rows, ds(plus(i, 1, h // 2), 1), hs(half)].rearrange("p a n -> p (a n)"),
                               ps(half, r0=64 * j, r1=64 * j + 64), ACT.Copy)
                act.wait_ge(sums_kept[j], plus(i, 16, 8 * (h - j) + 16))
                act.activation(sums[srow:srow + 1, hs(half)], ps(half, r0=srow, r1=srow + 1), ACT.Copy).then_inc(o_out, 1)
            for s in range(NB + 3):
                if s < NB:
                    half, t, q0, q1 = BLOCKS[s]
                    act.wait_ge(sc_sum, c(NB, s + 1))
                    act.wait_ge(p_lo_s, c(NB, s + 1))
                    act.activation(p_f[s % 4][:, 0:q1 - q0], ps(2 + s % 2, 0, q1 - q0), ACT.Exp,
                                   scale=SM).then_inc(p_exp, 1)
                if follow:
                    act_prep(act, s, h + 1, 1 - j, i)
                if s == 7:
                    leave(0)
            leave(1)
            act.wait_ge(o_out, c(2, 4))
            act.dma_start(sums_dram[ds(plus(i, 2, h), 1), :], sums[srow:srow + 1, :]).then_inc(sums_kept[j], 16)

        def dve_head(dve, h, j, i, follow):
            for s in range(NB + 3):
                if s < NB:
                    half, t, q0, q1 = BLOCKS[s]
                    dve.wait_ge(p_exp, plus(i, 2 * NB, NB * h + s + 3))
                    if q0 == P * t:
                        V.link(dve.memset(p_f[s % 4][64:128, 0:CHUNK], 0.0))
                    dve.wait_ge(pv_done, plus(i, 2 * NB, NB * h + s + 1))
                    dve.tensor_copy(p_hi[s % 4][:, 0:q1 - q0], p_f[s % 4][:, 0:q1 - q0]).then_inc(p_hi_s, 1)
                if follow:
                    dve_prep(dve, s, h + 1, 1 - j, i)

        def pool_head(pool, h, j, i, follow):
            for s in range(NB):
                half, t, q0, q1 = BLOCKS[s]
                pool.wait_ge(p_hi_s, plus(i, 2 * NB, NB * h + s + 1))
                pool.tensor_tensor(p_lo[s % 4][:, 0:q1 - q0], p_f[s % 4][:, 0:q1 - q0], f(p_hi[s % 4][:, 0:q1 - q0]),
                                   ALU.subtract).then_inc(p_lo_s, 1)
                if follow and s == 6:
                    pool_w(pool, (U_MLA + 1 - j) % 2, plus(i, 2, U_MLA + h + 3))

        def mla_heads(eng, head, prep_step, steps=None):
            for s in range(NB + 1):
                if s == 5 and prep_step is pe_prep:
                    pe_v_ready(eng, 0, None)
                prep_step(eng, s, 0, 0, None)
            with eng.Fori(0, MLA_HEADS // 2 - 1) as i:
                if steps:
                    steps.enter(i, 2 * (8 + PREP_V))
                head(eng, 0, 0, i, True)
                head(eng, 1, 1, i, True)
                if steps:
                    steps.leave(MLA_HEADS // 2 - 1)
            head(eng, MLA_HEADS - 2, 0, None, True)
            head(eng, MLA_HEADS - 1, 1, None, False)

        def pool_prep(pool, s, h, j, i):
            if s == 4:
                pool_w(pool, (U_MLA + j) % 2, U_MLA + h + 2)

        def all_kept(eng):
            eng.wait_ge(sums_back, 16)

        def pe_mla_norm(pe):
            pe.wait_ge(sel_s, 3)
            pe.wait_ge(o_out, 2 * MLA_HEADS + 2)
            for m in range(KT):
                if m >= 4:
                    pe.wait_ge(on_s, m - 3)
                for half in range(2):
                    pe.wait_ge(rec_s, half + 1)
                    last = pe.matmul(ps(2 * (m % 4) + half), select[:, blk(m)], recip[:, hs(half)], start=True, stop=True)
                last.then_inc(bc_sum, 1)
            pe.wait_ge(ol_s, KT)

        def dve_mla_norm(dve):
            all_kept(dve)
            for half in range(2):
                dve.reciprocal(recip[:, hs(half)], sums_all[:, hs(half)]).then_inc(rec_s, 1)
            for m in range(KT):
                dve.wait_ge(bc_sum, m + 1)
                dve.tensor_tensor(o_un[:, m, :], o_un[:, m, :], pair(2 * (m % 4)), ALU.mult).then_inc(on_s, 1)
                if m:
                    low(dve, m - 1)
            low(dve, KT - 1)

        def low(dve, m):
            dve.wait_ge(oh_s, m + 1)
            dve.tensor_tensor(a_lo[:, m, :], o_un[:, m, :], f(a_hi[:, m, :]), ALU.subtract).then_inc(ol_s, 1)

        def act_mla_norm(act):
            for j in range(2):
                act.wait_ge(sums_kept[j], 16 * MLA_HEADS // 2 + 16)
            act.dma_start(sums_all[:], sums_dram).then_inc(sums_back, 16)
            for m in range(KT):
                act.wait_ge(on_s, m + 1)
                act.activation(a_hi[:, m, :], o_un[:, m, :], ACT.Copy).then_inc(oh_s, 1)
            act.wait_ge(ol_s, KT)
            act.dma_start(x[:], x_mid).then_inc(x_loaded[2], 16)

        def pool_select(pool):
            all_kept(pool)
            pool.memset(select[:], 1.0).then_inc(sel_s, 1)
            pool.wait_ge(sel_s, 1)
            pool.affine_select(out=select[:], in_=select[:], compare_op=ALU.is_ge, fill=0.0, base=0,
                               pattern=[[1, S]], channel_multiplier=-MLA_V).then_inc(sel_s, 1)
            pool.wait_ge(sel_s, 2)
            pool.affine_select(out=select[:], in_=select[:], compare_op=ALU.is_ge, fill=0.0, base=MLA_V - 1,
                               pattern=[[-1, S]], channel_multiplier=MLA_V).then_inc(sel_s, 1)

        Y_DONE = [(out_free[0], KT + 2), (down_free[0], 8 * NFB + 2), (out_free[1], KT + 2), (down_free[1], 8 * NFB + 2)]

        with nc.Block() as block:
            @block.sync
            def _(sp):
                def load(j, u):
                    sp.dma_start(w_raw[j][:], units[ds(u, 1)].rearrange("a p n -> p (a n)")).then_inc(w_loaded[j], 16)
                sp.dma_start(x[:], x_in).then_inc(x_loaded[0], 16)
                sp.dma_start(col[:], cols).then_inc(par_in, 16)
                sp.dma_start(gate_all[:], gate_up).then_inc(par_in, 16)
                for u in range(2):
                    load(u, u)
                with sp.Fori(0, (UNITS - 2) // 2) as i:
                    for d in range(2):
                        sp.wait_ge(lo_ready, i * 2 + (d + 1))
                        load(d, i * 2 + (d + 2))
                for u in range(UNITS - (UNITS - 2) % 2, UNITS):
                    sp.wait_ge(lo_ready, u - 1)
                    load(u % 2, u)
                for half in range(2):
                    sp.wait_ge(x_new[3], KT * (half + 1))
                    sp.dma_start(out[:, :, hs(half)], x[:, :, hs(half)]).then_inc(stored, 16)
                sp.wait_ge(stored, 32)

            @block.gpsimd
            def _(pool):
                pool.memset(ones[:], 1.0).then_inc(consts, 1)
                pool.memset(eps[:], EPS).then_inc(consts, 1)
                pool.memset(halfpi[:], 1.5707963267948966).then_inc(consts, 1)
                pool.memset(ident[:], 0.0).then_inc(consts, 1)
                pool.wait_ge(consts, 4)
                pool.affine_select(out=ident[:], in_=ident[:], compare_op=ALU.not_equal, fill=1.0, base=0,
                                   pattern=[[-1, P]], channel_multiplier=1).then_inc(consts, 1)
                for u in range(2):
                    pool_w(pool, u, u)
                pool_pre(pool, 0)
                pool_w(pool, U_GLR % 2, U_GLR + 2)
                pool_units(pool, U_GLA, U_MLP0 - U_GLA)

                def zero_y(n):
                    pool.wait_ge(x_new[n], 2 * KT)
                    pool.memset(y[:], 0.0).then_inc(y_zeroed, 1)
                zero_y(0)
                pool_pre(pool, 1)
                pool_units(pool, U_MLP0, MLP_UNITS)
                pool_pre(pool, 2)
                pool_units(pool, U_MLA_IN, MLA_IN_UNITS)
                pool_pads(pool)
                pool.sem_inc(p_lo_s, 4)
                mla_heads(pool, pool_head, pool_prep)
                pool_select(pool)
                pool_units(pool, U_MLA_OUT, KT)
                zero_y(2)
                pool_pre(pool, 3)
                pool_units(pool, U_MLP1, MLP_UNITS - 2)

            @block.scalar
            def _(act):
                nonlocal AC
                AC = Steps(act, act_s)
                act.dma_start(cond[:], cond_in).then_inc(cond_loaded, 16)
                act.dma_start(ada_first[:], ada[0:ADA_FIRST].rearrange("a p n -> p a n")).then_inc(ada_in, 16)
                act_ada_load(act, ADA_FIRST % 2, ADA_FIRST)
                act.wait_ge(cond_loaded, 16)
                act.activation(cond[:], cond[:], ACT.Silu).then_inc(cond_ready, 1)
                for u in range(2):
                    act_w(act, u, u)
                act.wait_ge(consts, 5)
                act.wait_ge(x_loaded[0], 16)
                act_bridge(act, None, False, 1)
                act_gla(act)
                act_out(act, 0, U_GLA_OUT, True)
                act_bridge(act, 0, True, 2)
                act_mlp(act, 0, U_MLP0, True)
                act_bridge(act, 1, True, 3)
                act_mla_in(act)
                act.sem_inc(p_exp, 2)
                act.sem_inc(o_out, 2)
                for j in range(2):
                    act.sem_inc(sums_kept[j], 16)
                mla_heads(act, act_head, act_prep)
                act_mla_norm(act)
                act_out(act, 1, U_MLA_OUT, False)
                act_bridge(act, 2, True, 4)
                act_mlp(act, 1, U_MLP1, False)
                act_bridge(act, 3, True, 0)

            @block.vector
            def _(dve):
                nonlocal V
                V = Steps(dve, dve_s)

                def fold(count, *which):
                    for n, what in which:
                        dve_fold(dve, n, what)
                    dve.wait_ge(folded, count)
                dve.wait_ge(par_in, 32)
                dve.wait_ge(cond_ready, 1)
                dve.wait_ge(ada_in, 16)
                for a in range(ADA_FIRST):
                    dve_ada(dve, V, a % 2, a, ada_first[:, a, :])
                dve.wait_ge(ada_done, ADA_FIRST)
                fold(1, (0, "scale"))
                dve.wait_ge(consts, 5)
                dve_bridge(dve, None, False, 1)
                dve_gla(dve)
                dve_out_adas(dve)
                dve.wait_ge(ada_done, 6 * KT)
                fold(4, (0, "gate"), (1, "scale"), (1, "gate"))
                dve_bridge(dve, 0, True, 2)
                dve_mlp(dve, 0, U_MLP0, True)
                dve.wait_ge(ada_done, N_ADA)
                fold(8, (2, "scale"), (2, "gate"), (3, "scale"), (3, "gate"))
                dve_bridge(dve, 1, True, 3)
                dve_mla_in(dve)
                mla_heads(dve, dve_head, dve_prep, V)
                dve_mla_norm(dve)
                dve_bridge(dve, 2, True, 4)
                dve_mlp(dve, 1, U_MLP1, False)
                dve_bridge(dve, 3, True, 0)

            @block.tensor
            def _(pe):
                pe.wait_ge(consts, 5)
                pe_bridge(pe, None, False, 1)
                pe.wait_ge(PRE[0].lo, 2 * KT)
                pe_gla(pe)
                pe_out(pe, 0, U_GLA_OUT)
                pe_bridge(pe, 0, True, 2)
                pe.wait_ge(PRE[1].lo, 2 * KT)
                pe_mlp(pe, 0, U_MLP0)
                pe_bridge(pe, 1, True, 3)
                pe.wait_ge(PRE[2].lo, 2 * KT)
                pe_mla_in(pe)
                pe.wait_ge(c_lo_s, QT + KVT)
                pe.wait_ge(ident_s, 1)
                pe.sem_inc(pv_done, 4)
                mla_heads(pe, pe_head, pe_prep)
                pe_mla_norm(pe)
                pe_out(pe, 1, U_MLA_OUT)
                pe_bridge(pe, 2, True, 4)
                pe.wait_ge(PRE[3].lo, 2 * KT)
                pe_mlp(pe, 1, U_MLP1)
                pe_bridge(pe, 3, True, 0)


def kernel(**inputs):
    import numpy as np
    import concourse.bacc as bacc
    from concourse.bass_utils import run_bass_kernel_spmd as run

    g = {k: np.asarray(v) for k, v in inputs.items()}

    def tiles(w):
        k, m = w.shape
        return w.reshape(k // P, P, m // P, P).transpose(2, 1, 0, 3).reshape(m // P, P, k)

    def padded(w, n):
        return np.concatenate([w, np.zeros((w.shape[0], n - w.shape[1]), w.dtype)], axis=1)

    def mlp(layer):
        up = tiles(g["mlp_w_up"][layer]).reshape(NFB, 2, P, 1024)
        down = g["mlp_w_down"][layer].reshape(NFB, 2, P, 2, 4, P).transpose(0, 3, 2, 4, 1, 5).reshape(NFB, 2, P, 1024)
        order = [up[0]]
        for b in range(1, NFB):
            order += [up[b], down[b - 1]]
        return np.concatenate(order + [down[NFB - 1]])

    w = g["gla_w_in"][0]
    kw, vw = GLA_HEADS * GLA_DK, GLA_HEADS * GLA_DV
    wq, wk, wv, wr, wg = np.split(w, [kw, 2 * kw, 2 * kw + vw, 2 * kw + 2 * vw], axis=1)
    q, k, v, r = tiles(wq), tiles(wk), tiles(wv), tiles(wr)
    parts = [tiles(padded(wg, P))]
    for h in range(GLA_HEADS):
        parts += [k[h:h + 1], v[2 * h:2 * h + 2], q[h:h + 1], r[2 * h:2 * h + 2]]
    parts += [tiles(g["gla_w_out"][0]), mlp(0)]
    w = g["mla_w_in"][0]
    half = ROPE // 2
    kr = w[:, Q_RANK + KV_RANK:]
    zero = np.zeros((D, NOPE), w.dtype)
    parts += [tiles(w[:, :Q_RANK + KV_RANK]), tiles(np.concatenate([zero, kr, kr[:, half:], kr[:, :half]], axis=1))]
    wq = g["mla_w_uq"][0].reshape(QT, P, MLA_HEADS, NOPE + ROPE)
    wq = np.concatenate([wq, wq[..., NOPE + half:], wq[..., NOPE:NOPE + half]], axis=-1)
    wkv = g["mla_w_ukv"][0].reshape(KVT, P, MLA_HEADS, NOPE + MLA_V)
    heads = np.concatenate([wq, wkv, np.zeros((KT - QT - KVT, P, MLA_HEADS, P), wq.dtype)], axis=0)
    parts += [heads.transpose(2, 1, 0, 3).reshape(MLA_HEADS, P, 1024), tiles(g["mla_w_out"][0]), mlp(1)]
    units = np.ascontiguousarray(np.concatenate(parts))
    assert units.shape == (UNITS, P, 1024)

    def columns(v):
        return v.reshape(-1, P).T
    freq = (np.float32(THETA) ** (-np.arange(half, dtype=np.float32) / half)).astype(np.float32)
    sign = np.repeat(np.array([-1.0, 1.0], np.float32), half)
    place = np.zeros((P, 2), np.float32)
    place[NOPE:NOPE + ROPE, 0] = np.tile(freq, 2)
    place[NOPE:NOPE + ROPE, 1] = sign
    cols = np.ascontiguousarray(np.concatenate([
        columns(g["ada_b"]), columns(g["norm_pre_g"]), columns(g["norm_post_g"]), columns(g["gla_b_gate"]),
        columns(g["gla_head_g"]), columns(g["mla_q_norm_g"]), columns(g["mla_kv_norm_g"]), place], axis=1))
    arrays = {
        "x_in": np.ascontiguousarray(g["x"][0].T.reshape(KT, P, S).transpose(1, 0, 2)),
        "units": units,
        "ada": np.ascontiguousarray(g["ada_w"].transpose(0, 2, 1).reshape(N_ADA, P, D)),
        "cols": cols,
        "cond_in": np.ascontiguousarray(np.broadcast_to(g["c"], (P, D))),
        "gate_up": np.ascontiguousarray(g["gla_w_gate_up"][0]),
        "pos_in": np.ascontiguousarray(np.broadcast_to(g["positions"][0], (ROPE, S))),
    }
    nc = bacc.Bacc("TRN2", target_bir_lowering=False, num_devices=1)
    args = [nc.dram_tensor(n, a.shape, mybir.dt.from_np(a.dtype), kind="ExternalInput").ap() for n, a in arrays.items()]
    x_mid = nc.dram_tensor("x_mid", (P, KT, S), F32, kind="Internal").ap()
    sums = nc.dram_tensor("sums", (MLA_HEADS, S), F32, kind="Internal").ap()
    out = nc.dram_tensor("out", (P, KT, S), F32, kind="ExternalOutput").ap()
    build(nc, *args, x_mid, sums, out)
    res = run(nc, [arrays], core_ids=[0]).results[0]["out"]
    return np.ascontiguousarray(res.transpose(1, 0, 2).reshape(1, D, S).transpose(0, 2, 1))
```

```python
from contextlib import ExitStack

import concourse.bass as bass
from concourse import mybir

F32 = mybir.dt.float32
F32R = mybir.dt.float32r
I32 = mybir.dt.int32
ACT = mybir.ActivationFunctionType
ALU = mybir.AluOpType
AX = mybir.AxisListType.X
ds = bass.ds

P = 128
D = 1024
S = 1024
DEPTH = 2
HALF = 512
KT = D // P
CHUNK = 64
EPS = 1e-6

GLA_HEADS, GLA_DK, GLA_DV, GLA_RANK, GLA_TEMP = 4, 128, 256, 16, 16.0
NCH = S // CHUNK
MLA_HEADS, NOPE, ROPE, MLA_V, Q_RANK, KV_RANK = 16, 64, 32, 64, 384, 256
QT, KVT = Q_RANK // P, KV_RANK // P
THETA = 10000.0
D_FF = 4 * D
FB = 256
NFB = D_FF // FB

GLA_PER_HEAD = 6
U_GLR = 0
U_GLA = 1
U_GLA_OUT = U_GLA + GLA_PER_HEAD * GLA_HEADS
U_MLP0 = U_GLA_OUT + KT
MLP_UNITS = 2 * D * D_FF // (P * 1024)
U_MLA_IN = U_MLP0 + MLP_UNITS
MLA_IN_UNITS = QT + KVT + 1
U_MLA = U_MLA_IN + MLA_IN_UNITS
U_MLA_OUT = U_MLA + MLA_HEADS
U_MLP1 = U_MLA_OUT + KT
UNITS = U_MLP1 + MLP_UNITS

N_ADA = DEPTH * 6 * KT
C_PRE = N_ADA
C_POST = C_PRE + 2 * DEPTH * KT
C_BGATE = C_POST + 2 * DEPTH * KT
C_HEADG = C_BGATE + GLA_HEADS
C_QG = C_HEADG + GLA_DV // P
C_KVG = C_QG + QT
C_FREQ = C_KVG + KVT
C_SIGN = C_FREQ + 1
NCOL = C_SIGN + 1
ADA_FIRST = 2 * KT
PI = 3.1415925
TWO_PI = (6.28125, 1.9350051879882812e-03, 3.019916050561733e-07)
ROUND = 1.5 * 2.0 ** 23


class Steps:

    def __init__(self, eng, sem):
        self.eng, self.sem, self.base, self.k, self.per, self.i = eng, sem, 0, 0, 0, None

    def mark(self, ins):
        self.k += 1
        ins.then_inc(self.sem, 1)
        return self.at()

    def at(self):
        return self.base + self.k + (self.i * self.per if self.i is not None else 0)

    def link(self, ins):
        self.eng.wait_ge(self.sem, self.mark(ins))

    def enter(self, i, per):
        self.base, self.k, self.i, self.per = self.base + self.k, 0, i, per

    def leave(self, trips):
        assert self.k == self.per, f"{self.k} steps in a loop said to have {self.per}"
        self.base, self.k, self.i = self.base + self.per * trips, 0, None


def build(nc, x_in, units, ada, cols, cond_in, gate_up, pos_in, x_mid, sums_dram, out):
    ctx = ExitStack()
    AC = V = None
    with ctx:
        def sem(name):
            return ctx.enter_context(nc.semaphore(name))

        base = (nc.sbuf_base + 31) // 32 * 32
        KB = 1024

        def at(name, off, shape, dt=F32):
            return nc.alloc_sbuf_tensor_at(name, shape, dt, offset=base + off)

        X, WR, A, H, Y, T, M = 0, 32 * KB, 56 * KB, 120 * KB, 152 * KB, 184 * KB, 192 * KB
        C = 204 * KB
        x = at("x", X, [P, KT, S])
        w_raw = [at(f"w_raw{j}", WR + j * 4 * KB, [P, 1024]) for j in range(2)]
        w_hi = [at(f"w_hi{j}", WR + (8 + 4 * j) * KB, [P, 1024], F32R) for j in range(2)]
        w_lo = [at(f"w_lo{j}", WR + (16 + 4 * j) * KB, [P, 1024], F32R) for j in range(2)]
        a_hi = at("a_hi", A, [P, KT, S], F32R)
        a_lo = at("a_lo", A + 32 * KB, [P, KT, S], F32R)
        ada_first = at("ada_first", A, [P, ADA_FIRST, D])
        y = at("y", Y, [P, KT, S])
        ada_raw = [at(f"ada_raw{j}", M + j * 4 * KB, [P, D]) for j in range(2)]
        cond = at("cond", M + 8 * KB, [P, D])
        ident = at("ident", C, [P, P])
        ones = at("ones", C + 512, [P, P])
        col = at("col", C + 1024, [P, NCOL])
        mod = at("mod", C + 1792, [P, N_ADA])
        acc = at("acc", C + 2176, [P, 2])
        eps = at("eps", C + 2208, [P, 1])
        halfpi = at("halfpi", C + 2240, [P, 1])
        gla_b = at("gla_b", C + 2272, [P, 1])
        dec = at("dec", C + 2304, [P, NCH])
        mx = at("mx", C + 2368, [P, 8])
        mx2 = at("mx2", C + 2400, [P, 8])
        mx_r = at("mx_r", C + 2432, [P, 8], F32R)
        ysq = [at(f"ysq{j}", H + 4 * j * KB, [P, S]) for j in range(2)]
        ysum = at("ysum", H + 8 * KB, [P, S])
        rstd_y = at("rstd_y", H + 12 * KB, [P, S])
        nt = [at(f"nt{j}", H + (16 + 2 * j) * KB, [P, HALF]) for j in range(4)]
        sq = [at(f"sq{j}", H + (24 + 2 * j) * KB, [P, HALF]) for j in range(4)]
        nv = [at(f"nv{j}", T + 2 * j * KB, [P, HALF]) for j in range(4)]
        rstd_x = at("rstd_x", H, [P, S])
        hid_hi = [at(f"hid_hi{j}", H + j * 16 * KB, [P, 2, S], F32R) for j in range(2)]
        hid_lo = [at(f"hid_lo{j}", H + (8 + j * 16) * KB, [P, 2, S], F32R) for j in range(2)]
        relu = [at(f"relu{j}", T + j * 4 * KB, [P, S]) for j in range(2)]
        o_all = at("o_all", X, [P, KT, S])
        g_hi = at("g_q_hi", H, [P, S], F32R)
        g_lo = at("g_q_lo", H + 4 * KB, [P, S], F32R)
        g_k = at("g_k", H + 8 * KB, [P, S])
        g_v = at("g_v", H + 12 * KB, [P, 2, S])
        tok_hi = at("tok_hi", H + 20 * KB, [P, 8, 384], F32R)
        tok_lo = at("tok_lo", H + 32 * KB, [P, 8, 384], F32R)
        g_r = at("g_r", H + 44 * KB, [P, 2, S])
        g_t1 = at("g_t1", H + 52 * KB, [P, S])
        g_t2 = at("g_t2", H + 56 * KB, [P, S])
        o_tok = at("o_tok", H + 52 * KB, [P, 8, GLA_DV])
        o_sq = at("o_sq", H + 12 * KB, [P, 8, GLA_DV])
        glr = at("glr", H + 60 * KB, [GLA_RANK, S])
        st = [at(f"st{j}", H + (64 + j) * KB, [P, GLA_DV]) for j in range(2)]
        st_hi = [at(f"st_hi{j}", H + (66 + j) * KB, [P, GLA_DV], F32R) for j in range(2)]
        st_lo = [at(f"st_lo{j}", H + (68 + j) * KB, [P, GLA_DV], F32R) for j in range(2)]
        gate_all = at("gate_all", H + 70 * KB, [GLA_RANK, GLA_HEADS * GLA_DK])
        gate_w = at("gate_w", C + 2464, [GLA_RANK, GLA_DK])
        o_un = at("o_un", X, [P, KT, S])
        c_f = at("c_f", X, [P, QT + KVT, S])
        krope = at("krope", X + 20 * KB, [P, S])
        rstd_q = at("rstd_q", X + 24 * KB, [P, S])
        rstd_kv = at("rstd_kv", X + 28 * KB, [P, S])
        c_hi = at("c_hi", H, [P, QT + KVT, S], F32R)
        c_lo = at("c_lo", H + 20 * KB, [P, QT + KVT, S], F32R)
        p_f = [at(f"p_f{j}", H + (40 + 2 * j) * KB, [P, HALF]) for j in range(4)]
        p_hi = [at(f"p_hi{j}", H + (48 + 2 * j) * KB, [P, HALF], F32R) for j in range(4)]
        p_lo = [at(f"p_lo{j}", H + (56 + 2 * j) * KB, [P, HALF], F32R) for j in range(4)]
        sums = at("sums", T, [P, S])
        sums_all = at("sums_all", T + 4 * KB, [MLA_HEADS, S])
        k_hi = [at(f"k_hi{j}", A + (8 * j) * KB, [P, S], F32R) for j in range(2)]
        k_lo = [at(f"k_lo{j}", A + (8 * j + 4) * KB, [P, S], F32R) for j in range(2)]
        q_hi = [at(f"q_hi{j}", A + (16 + 8 * j) * KB, [P, S], F32R) for j in range(2)]
        q_lo = [at(f"q_lo{j}", A + (20 + 8 * j) * KB, [P, S], F32R) for j in range(2)]
        v_hi = [at(f"v_hi{j}", A + (32 + 8 * j) * KB, [P, 8, P], F32R) for j in range(2)]
        v_lo = [at(f"v_lo{j}", A + (36 + 8 * j) * KB, [P, 8, P], F32R) for j in range(2)]
        q_f = at("q_f", A + 48 * KB, [P, S])
        v_f = at("v_f", A + 52 * KB, [P, S])
        ident_r = at("ident_r", M, [P, P], F32R)
        rope_t = at("rope_t", M + 512, [P, HALF])
        cos_t = at("cos_t", M + 2560, [P, S])
        sin_t = at("sin_t", M + 2560 + 4 * KB, [P, S])
        ang = at("ang", H + 40 * KB, [P, S])
        turns = at("turns", H + 44 * KB, [P, S])
        pos_i = at("pos_i", H + 48 * KB, [P, S], I32)
        c_sq = [at(f"c_sq{j}", H + (52 + 2 * j) * KB, [P, HALF]) for j in range(4)]
        select = at("select", H + 40 * KB, [MLA_HEADS, S])
        recip = at("recip", H + 44 * KB, [MLA_HEADS, S])

        psum = ctx.enter_context(nc.psum_tensor("psum", [P, 8, HALF], F32))

        def ps(bank, c0=0, c1=HALF, r0=0, r1=P):
            return psum[r0:r1, bank, c0:c1]

        def pair(b, r0=0, r1=P):
            return psum[r0:r1, b:b + 2, :].rearrange("p a b -> p (a b)")

        def f(rounded):
            return rounded.bitcast(F32)

        def hs(half):
            return slice(half * HALF, (half + 1) * HALF)

        def blk(k):
            return slice(k * P, (k + 1) * P)

        def wait(eng, s, n):
            if not isinstance(n, int) or n > 0:
                eng.wait_ge(s, n)

        par_in = sem("parameters_loaded")
        cond_loaded, gate_in = sem("cond_loaded"), sem("gate_weights_loaded")
        x_loaded = [sem(f"x_loaded{n}") for n in range(DEPTH + 1)]
        x_spilled = sem("x_spilled")
        stored = sem("out_stored")
        consts = sem("constants_made")
        w_loaded = [sem(f"w_loaded{j}") for j in range(2)]
        hi_ready = sem("w_hi_ready")
        lo_ready = sem("w_lo_ready")
        unit_done = sem("unit_done")
        ADA_PART = ADA_FIRST // 4
        ada_in = [sem(f"ada_first_loaded{n}") for n in range(4)]
        ada_loaded = [sem(f"ada_loaded{j}") for j in range(2)]
        ada_done = sem("ada_done")
        cond_ready = sem("cond_ready")
        act_s, dve_s = sem("act_steps"), sem("dve_steps")

        class Norm:

            def __init__(self, name):
                self.squared = sem(f"{name}_squared")
                self.summed = sem(f"{name}_summed")
                self.rstd = sem(f"{name}_rstd")

        class Pre:

            def __init__(self, name):
                self.scaled = sem(f"{name}_scaled")
                self.hi = sem(f"{name}_hi")
                self.lo_pool = sem(f"{name}_lo_by_pool")
                self.lo_dve = sem(f"{name}_lo_by_dve")

            def wait_lo(self, eng, m, half):
                wait_share(eng, m, KT * half + KT - 1, self.lo_pool, self.lo_dve)
                wait_share(eng, m, KT * half + KT - 2, self.lo_pool, self.lo_dve)

        EACH = 2 * KT
        NX, PRE = Norm("norm_x"), Pre("pre")
        ny_summed, ny_rstd = sem("norm_y_summed"), sem("norm_y_rstd")
        ITEMS = [(half, k) for half in range(2) for k in range(KT)]
        y_squared = [sem(f"y_squared{n}") for n in range(4)]
        y_sq_added = [sem(f"y_squares_added{n}") for n in range(4)]
        step_made, x_pool, x_dve = sem("x_step"), sem("x_updated_by_pool"), sem("x_updated_by_dve")
        POOL_K = (0, 2, 3, 5, 6)

        def share(idx):
            ks = [k for _, k in ITEMS[:idx + 1]]
            pool = sum(k in POOL_K for k in ks)
            return pool, len(ks) - pool

        def wait_share(eng, n, idx, pool_sem, dve_sem):
            if idx >= 0:
                every = share(EACH - 1)
                if ITEMS[idx][1] in POOL_K:
                    eng.wait_ge(pool_sem, n * every[0] + share(idx)[0])
                else:
                    eng.wait_ge(dve_sem, n * every[1] + share(idx)[1])

        y_zeroed = sem("y_zeroed")
        folded = sem("modulations_folded")

        def sub(n):
            b = n * 3 * KT
            return b, b + KT, b + 2 * KT

        def act_w(act, j, u):
            if not isinstance(u, int) or u < UNITS:
                wait(act, unit_done, u - 1)
                act.wait_ge(w_loaded[j], (u - j) * 8 + 16)
                act.activation(w_hi[j][:], w_raw[j][:], ACT.Copy).then_inc(hi_ready, 1)

        def pool_w(pool, j, u):
            if not isinstance(u, int) or u < UNITS:
                pool.wait_ge(hi_ready, u + 1)
                pool.tensor_tensor(w_lo[j][:], w_raw[j][:], f(w_hi[j][:]), ALU.subtract).then_inc(lo_ready, 1)

        def pool_units(pool, u, n):
            with pool.Fori(0, n // 2) as i:
                for d in range(2):
                    pool_w(pool, (u + d) % 2, i * 2 + (u + d + 2))

        def dve_ada(dve, V, j, a, buf):
            V.link(dve.scalar_tensor_tensor(out=buf, in0=buf, scalar=1.0, in1=cond[:], op0=ALU.mult,
                                            op1=ALU.mult, accum_out=acc[:, j:j + 1]))
            dve.tensor_tensor(mod[:, ds(a, 1)], acc[:, j:j + 1], col[:, ds(a, 1)], ALU.add).then_inc(ada_done, 1)

        def dve_ada_ring(dve, V, j, a):
            dve.wait_ge(ada_loaded[j], (a - ADA_FIRST - j) * 8 + 16)
            dve_ada(dve, V, j, a, ada_raw[j][:])

        def act_ada_load(act, j, a):
            if not isinstance(a, int) or a < N_ADA:
                if not isinstance(a, int) or a >= ADA_FIRST + 2:
                    act.wait_ge(ada_done, a - 1)
                act.dma_start(ada_raw[j][:], ada[ds(a, 1)].rearrange("a p n -> p (a n)")).then_inc(ada_loaded[j], 16)

        def act_squares(act, nm, src, items, ring):
            for n, (half, k) in enumerate(items):
                wait(act, nm.summed, n - len(ring) + 1)
                act.activation(ring[n % len(ring)][:], src[:, k, hs(half)], ACT.Square).then_inc(nm.squared, 1)

        def act_rstd(act, summed, rstd, half, bank, dst, width, seen):
            act.wait_ge(summed, seen)
            AC.link(act.activation(dst[:, hs(half)], ps(bank), ACT.Ln, bias=eps[:], scale=1.0 / width))
            act.activation(dst[:, hs(half)], dst[:, hs(half)], ACT.Exp, scale=-0.5).then_inc(rstd, 1)

        def pe_sums(pe, nm, items, ring, bank, first, last, before=0):
            for n, (half, k) in enumerate(items):
                pe.wait_ge(nm.squared, before + n + 1)
                pe.matmul(ps(bank + half), ones[:], ring[n % len(ring)][:], start=(k == first),
                          stop=(k == last)).then_inc(nm.summed, 1)

        def act_y_square(act, n, t, src):
            act.wait_ge(y_sq_added[n], t + 1)
            act.activation(ysq[t % 2][:], src, ACT.Square).then_inc(y_squared[n], 1)

        def pool_y_sum(pool, n, t):
            if 0 < t < KT - 1:
                pool.wait_ge(y_squared[n], t + 1)
                if t > 1:
                    pool.wait_ge(y_sq_added[n], t + 1)
                pool.tensor_tensor(ysum[:], (ysum if t > 1 else ysq[0])[:], ysq[t % 2][:], ALU.add).then_inc(y_sq_added[n], 1)

        def pe_bridge(pe, n, post, pre, bank):
            if post:
                for part, s_, c in ((ysum, y_sq_added[n], KT), (ysq[(KT - 1) % 2], y_squared[n], KT)):
                    pe.wait_ge(s_, c)
                    for half in range(2):
                        last = pe.matmul(ps(bank + half), ones[:], part[:, hs(half)], start=(part is ysum),
                                         stop=(part is not ysum))
                last.then_inc(ny_summed, 1)
            if pre:
                if post:
                    pe.wait_ge(*Y_DONE[n])
                pe_sums(pe, NX, ITEMS, sq, bank + 2, 0, KT - 1, EACH * (pre - 1))

        def act_bridge(act, n, post, pre, bank, spill=None):
            if post:
                act.wait_ge(*Y_DONE[n])
                for half in range(2):
                    act_rstd(act, ny_summed, ny_rstd, half, bank + half, rstd_y, D, n + 1)
            if not pre:
                return
            m = pre - 1

            def square(idx):
                half, k = ITEMS[idx]
                if post:
                    wait_share(act, n, idx, x_pool, x_dve)
                wait(act, NX.summed, EACH * m + idx - 3)
                act.activation(sq[idx % 4][:], x[:, k, hs(half)], ACT.Square).then_inc(NX.squared, 1)

            def high(idx):
                half, k = ITEMS[idx]
                b = sub(m)[0] + k
                act.wait_ge(PRE.scaled, EACH * m + idx + 1)
                act.activation(a_hi[:, k, hs(half)], nv[idx % 4][:], ACT.Identity, bias=mod[:, b:b + 1])
                act.activation(nv[idx % 4][:], nv[idx % 4][:], ACT.Identity, bias=mod[:, b:b + 1]).then_inc(PRE.hi, 1)
            for idx in range(2 * KT):
                square(idx)
                if idx == KT + 1:
                    act_rstd(act, NX.summed, NX.rstd, 0, bank + 2, rstd_x, D, EACH * m + KT)
            if spill:
                spill(act)
            for idx in range(2 * KT):
                high(idx)
                if idx == 1:
                    act_rstd(act, NX.summed, NX.rstd, 1, bank + 3, rstd_x, D, EACH * (m + 1))

        def dve_bridge(dve, n, post, pre):
            if post:
                gate = sub(n)[2]
                if n in (0, 2):
                    dve.wait_ge(x_loaded[1 + n // 2], 16)
                for idx, (half, k) in enumerate(ITEMS):
                    if k == 0:
                        dve.wait_ge(ny_rstd, 2 * n + half + 1)
                    if idx >= 4:
                        wait_share(dve, n, idx - 4, x_pool, x_dve)
                    dve.scalar_tensor_tensor(out=nt[idx % 4][:], in0=y[:, k, hs(half)],
                                             scalar=mod[:, gate + k:gate + k + 1],
                                             in1=rstd_y[:, hs(half)], op0=ALU.mult, op1=ALU.mult).then_inc(step_made, 1)
                    if k not in POOL_K:
                        dve.wait_ge(step_made, EACH * n + idx + 1)
                        dve.tensor_tensor(x[:, k, hs(half)], x[:, k, hs(half)], nt[idx % 4][:],
                                          ALU.add).then_inc(x_dve, 1)
            if not pre:
                return
            m = pre - 1
            scale = sub(m)[1]

            def low(idx):
                if idx >= 0 and ITEMS[idx][1] not in POOL_K:
                    half, k = ITEMS[idx]
                    dve.wait_ge(PRE.hi, EACH * m + idx + 1)
                    dve.tensor_tensor(a_lo[:, k, hs(half)], nv[idx % 4][:], f(a_hi[:, k, hs(half)]),
                                      ALU.subtract).then_inc(PRE.lo_dve, 1)
            for idx, (half, k) in enumerate(ITEMS):
                if k == 0:
                    dve.wait_ge(NX.rstd, 2 * m + half + 1)
                wait_share(dve, m, idx - 4, PRE.lo_pool, PRE.lo_dve)
                if post:
                    wait_share(dve, n, idx, x_pool, x_dve)
                dve.scalar_tensor_tensor(out=nv[idx % 4][:], in0=x[:, k, hs(half)],
                                         scalar=mod[:, scale + k:scale + k + 1],
                                         in1=rstd_x[:, hs(half)], op0=ALU.mult, op1=ALU.mult).then_inc(PRE.scaled, 1)
                low(idx - 2)
            low(2 * KT - 2)
            low(2 * KT - 1)

        def pool_step(pool, n):
            if n in (0, 2):
                pool.wait_ge(x_loaded[1 + n // 2], 16)
            for idx, (half, k) in enumerate(ITEMS):
                if k in POOL_K:
                    pool.wait_ge(step_made, EACH * n + idx + 1)
                    pool.tensor_tensor(x[:, k, hs(half)], x[:, k, hs(half)], nt[idx % 4][:], ALU.add).then_inc(x_pool, 1)

        def pool_pre(pool, m):
            for idx, (half, k) in enumerate(ITEMS):
                if k in POOL_K:
                    pool.wait_ge(PRE.hi, EACH * m + idx + 1)
                    pool.tensor_tensor(a_lo[:, k, hs(half)], nv[idx % 4][:], f(a_hi[:, k, hs(half)]),
                                       ALU.subtract).then_inc(PRE.lo_pool, 1)

        def dve_fold(dve, n, which):
            _, scale, gate = sub(n)
            if which == "scale":
                dve.scalar_tensor_tensor(out=mod[:, scale:scale + KT], in0=mod[:, scale:scale + KT], scalar=1.0,
                                         in1=col[:, C_PRE + n * KT:C_PRE + (n + 1) * KT],
                                         op0=ALU.add, op1=ALU.mult).then_inc(folded, 1)
            else:
                dve.tensor_tensor(mod[:, gate:gate + KT], mod[:, gate:gate + KT],
                                  col[:, C_POST + n * KT:C_POST + (n + 1) * KT], ALU.mult).then_inc(folded, 1)

        def pe_first(pe, m, u, banks):
            for d in range(len(banks)):
                pe.wait_ge(lo_ready, u + d + 1)
            for half in range(2):
                PRE.wait_lo(pe, m, half)
                for d in range(len(banks)):
                    for k in range(KT):
                        for p, (w, a) in enumerate(((w_hi, a_hi), (w_hi, a_lo), (w_lo, a_hi))):
                            last = pe.matmul(ps(banks[d] + half), w[(u + d) % 2][:, blk(k)], a[:, k, hs(half)],
                                             start=(k == 0 and p == 0), stop=(k == KT - 1 and p == 2))
                    if half == 1:
                        last.then_inc(unit_done, 1)

        def pe_unit(pe, j, u, bank, between=None, parts=None):
            pe.wait_ge(lo_ready, u + 1)
            n = 0
            for k in range(KT):
                if parts:
                    pe.wait_ge(parts, k + 1)
                for p, (w, a) in enumerate(((w_hi, a_hi), (w_hi, a_lo), (w_lo, a_hi))):
                    for half in range(2):
                        last = pe.matmul(ps(bank + half), w[j][:, blk(k)], a[:, k, hs(half)],
                                         start=(k == 0 and p == 0), stop=(k == KT - 1 and p == 2))
                        n += 1
                        if between and n % 3 == 0:
                            between(n // 3 - 1)
            last.then_inc(unit_done, 1)

        out_free = [sem(f"out_bank_free{n}") for n in range(2)]

        def pe_out(pe, n, u0, parts):
            pe.sem_inc(out_free[n], 2)
            with pe.Fori(0, KT // 2) as i:
                for d in range(2):
                    pe.wait_ge(out_free[n], i * 2 + (d + 1))
                    pe_unit(pe, (u0 + d) % 2, i * 2 + (u0 + d), 2 * d, parts=parts if d == 0 else None)

        def act_out(act, n, u0, adas):
            b = 2 * n
            with act.Fori(0, KT // 2) as i:
                for d in range(2):
                    j, u = (u0 + d) % 2, i * 2 + (u0 + d)
                    act_w(act, j, u + 2)
                    if adas:
                        act_ada_load(act, (ADA_OUT + d + 1) % 2, i * 2 + (ADA_OUT + d + 1))
                    act.wait_ge(y_sq_added[b], i * 2 + (d + 1))
                    act.wait_ge(unit_done, u + 1)
                    act.activation(ysq[d][:], pair(2 * d), ACT.Square).then_inc(y_squared[b], 1)
                    act.activation(y[:, ds(i * 2 + d, 1), :].rearrange("p a n -> p (a n)"), pair(2 * d),
                                   ACT.Copy).then_inc(out_free[n], 1)

        def pool_out(pool, n, u0):
            for t in range(KT):
                pool_w(pool, (u0 + t) % 2, u0 + t + 2)
                pool_y_sum(pool, 2 * n, t)

        ADA_OUT = ADA_FIRST + GLA_PER_HEAD * GLA_HEADS

        def dve_out_adas(dve):
            with dve.Fori(0, KT // 2) as i:
                V.enter(i, 2)
                for d in range(2):
                    dve_ada_ring(dve, V, (ADA_OUT + d) % 2, i * 2 + (ADA_OUT + d))
                V.leave(KT // 2)

        relu_ready = [sem(f"relu_ready{n}") for n in range(2)]
        up_value = [sem(f"up_value{n}") for n in range(2)]
        up_hi = [sem(f"up_hi{n}") for n in range(2)]
        up_lo = [sem(f"up_lo{n}") for n in range(2)]
        down_sum = [sem(f"down_sum{n}") for n in range(2)]
        down_free = [sem(f"down_free{n}") for n in range(2)]

        def mlp_plan(run, loop):
            run("up", 0, 0, 0, None)
            with loop(0, NFB // 2 - 1) as i:
                run("up", 1, 1, 2, i)
                run("down", 0, 0, 4, i)
                run("up", 2, 0, 6, i)
                run("down", 1, 1, 8, i)
            e = 2 + 4 * (NFB - 2)
            run("up", NFB - 1, 1, e, None)
            run("down", NFB - 2, 0, e + 2, None)
            run("down", NFB - 1, 1, e + 4, None)

        def plus(i, step, c):
            return c if i is None else i * step + c

        def pe_mlp(pe, m, u0):
            def run(kind, b, par, n, i):
                if n == 0:
                    pe_first(pe, 2 * m + 1, u0, (0, 2))
                    return
                for d in range(2):
                    j, u = (u0 + n + d) % 2, plus(i, 8, u0 + n + d)
                    if kind == "up":
                        wait(pe, up_value[m], plus(i, 4, 2 * b + d - 1))
                        pe_unit(pe, j, u, 2 * d)
                        continue
                    pe.wait_ge(lo_ready, u + 1)
                    pe.wait_ge(up_lo[m], plus(i, 4, 2 * b + 2))
                    for q in range(4):
                        bank = 4 + 2 * (q % 2)
                        pe.wait_ge(down_free[m], plus(i, 16, 8 * b + 4 * d + q + 1))
                        for k in range(2):
                            for p, (w, a) in enumerate(((w_hi, hid_hi), (w_hi, hid_lo), (w_lo, hid_hi))):
                                for half in range(2):
                                    last = pe.matmul(ps(bank + half), w[j][:, blk(2 * q + k)],
                                                     a[par][:, k, hs(half)], start=(k == 0 and p == 0),
                                                     stop=(k == 1 and p == 2))
                        if q < 3:
                            last.then_inc(down_sum[m], 1)
                    last.then_inc(unit_done, 1)
            pe.sem_inc(down_free[m], 2)
            mlp_plan(run, pe.Fori)

        def act_mlp(act, m, u0, adas):
            def run(kind, b, par, n, i):
                for d in range(2):
                    j, u = (u0 + n + d) % 2, plus(i, 8, u0 + n + d)
                    if kind == "up":
                        act.wait_ge(unit_done, u + 1)
                        wait(act, up_lo[m], plus(i, 4, 2 * b + d - 1))
                        act.activation(relu[d][:], pair(2 * d), ACT.Relu).then_inc(relu_ready[m], 1)
                    act_w(act, j, u + 2)
                    if adas and d < ADA_AT.get((kind, b, par), (0, 0))[1]:
                        a = ADA_AT[kind, b, par][0] + d + 1
                        act_ada_load(act, a % 2, plus(i, 6, a))
                    if kind == "up":
                        act.wait_ge(up_value[m], plus(i, 4, 2 * b + d + 1))
                        act.activation(hid_hi[par][:, d, :], relu[d][:], ACT.Copy).then_inc(up_hi[m], 1)
                    elif b == NFB - 1:
                        for t in range(4 * d, 4 * d + 4):
                            act.wait_ge(down_free[m], 8 * b + t + 3)
                            act_y_square(act, 2 * m + 1, t, y[:, t, :])
            mlp_plan(run, act.Fori)

        def pool_mlp(pool, m, u0):
            def run(kind, b, par, n, i):
                for d in range(2):
                    j, u = (u0 + n + d) % 2, plus(i, 8, u0 + n + d)
                    pool_w(pool, j, u + 2)
                    if kind == "up":
                        pool.wait_ge(up_hi[m], plus(i, 4, 2 * b + d + 1))
                        pool.tensor_tensor(hid_lo[par][:, d, :], relu[d][:], f(hid_hi[par][:, d, :]),
                                           ALU.subtract).then_inc(up_lo[m], 1)
                    elif b == NFB - 1:
                        for t in range(4 * d, 4 * d + 4):
                            pool_y_sum(pool, 2 * m + 1, t)
            mlp_plan(run, pool.Fori)

        def dve_mlp(dve, m, u0, adas):
            def run(kind, b, par, n, i):
                if i is not None and (b, kind) == (1, "up"):
                    V.enter(i, 6 if adas else 0)
                for d in range(2):
                    u = plus(i, 8, u0 + n + d)

                    def column():
                        if adas and d < ADA_AT.get((kind, b, par), (0, 0))[1]:
                            a = ADA_AT[kind, b, par][0] + d
                            dve_ada_ring(dve, V, a % 2, plus(i, 6, a))
                    if kind == "up":
                        dve.wait_ge(relu_ready[m], plus(i, 4, 2 * b + d + 1))
                        dve.scalar_tensor_tensor(out=relu[d][:], in0=pair(2 * d), scalar=0.0, in1=relu[d][:],
                                                 op0=ALU.max, op1=ALU.mult).then_inc(up_value[m], 1)
                        if d == 0:
                            column()
                        continue
                    for q in range(4):
                        if q < 3:
                            dve.wait_ge(down_sum[m], plus(i, 12, 6 * b + 3 * d + q + 1))
                        else:
                            dve.wait_ge(unit_done, u + 1)
                        t = 4 * d + q
                        dve.tensor_tensor(y[:, t, :], y[:, t, :], pair(4 + 2 * (q % 2)), ALU.add).then_inc(down_free[m], 1)
                        if q == 1:
                            column()
                if i is not None and (b, kind) == (1, "down"):
                    V.leave(NFB // 2 - 1)
            dve.wait_ge(y_zeroed, m + 1)
            mlp_plan(run, dve.Fori)

        A1 = 6 * KT
        ADA_AT = {("up", 0, 0): (A1, 1), ("up", 1, 1): (A1 + 1, 1), ("down", 0, 0): (A1 + 2, 2),
                  ("up", 2, 0): (A1 + 4, 1), ("down", 1, 1): (A1 + 5, 2), ("up", NFB - 1, 1): (A1 + 43, 1),
                  ("down", NFB - 2, 0): (A1 + 44, 2), ("down", NFB - 1, 1): (A1 + 46, 2)}


        gw_ready, gate_sum, gate_ln, gate_cum, decay_ready, kend = (sem(f"gla_{s}") for s in (
            "gate_weights", "gate_sum", "gate_ln", "gate_cum", "decay", "k_end"))
        a_ev, q_hi_s, q_lo_s = sem("gla_evacuated"), sem("gla_q_hi"), sem("gla_q_lo")
        tok_sum, tok_hi_s, tok_lo_s = sem("gla_transposed"), sem("gla_tok_hi"), sem("gla_tok_lo")
        kv_sum, st_new, st_hi_s, st_lo_s, o_sum, o_ev = (sem(f"gla_{s}") for s in (
            "kv_sum", "state", "state_hi", "state_lo", "o_sum", "o_evacuated"))
        o_scaled, o_turned, o_gated = sem("gla_o_scaled"), sem("gla_o_transposed"), sem("gla_o_gated")
        o_hi_s, o_lo_s = sem("gla_o_hi"), sem("gla_o_lo")
        NG = Norm("gla_head")
        QSCALE = GLA_DK ** -0.5

        def pe_gla(pe):
            pe_first(pe, 0, U_GLR, (4,))
            with pe.Fori(0, GLA_HEADS) as i:
                def u(d):
                    return (U_GLA + d) % 2, i * GLA_PER_HEAD + (U_GLA + d)
                pe.wait_ge(gw_ready, i + 1)
                pe.wait_ge(a_ev, i * 4 + 1)

                def gate(c):
                    if c == 4:
                        pe.wait_ge(o_gated, i * 2 + 1)
                        for half in range(2):
                            last = pe.matmul(ps(4 + half), gate_w[:], glr[:, hs(half)], start=True, stop=True)
                        last.then_inc(gate_sum, 1)

                def turn(c):
                    if c % 2 == 1:
                        t = c // 2
                        if t == 0:
                            pe.wait_ge(a_ev, i * 4 + 3)
                            pe.wait_ge(o_gated, i * 2 + 2)
                        if t >= 2:
                            pe.wait_ge(tok_lo_s, i * 8 + (t - 1))
                        for n, src in enumerate((g_k[:, blk(t)], g_v[:, 0, blk(t)], g_v[:, 1, blk(t)])):
                            last = pe.transpose(ps(6 + t % 2, n * P, n * P + P), src, ident[:])
                        last.then_inc(tok_sum, 1)
                pe_unit(pe, *u(0), 0, between=gate)
                pe_unit(pe, *u(1), 2)
                pe.wait_ge(kend, i + 1)
                pe_unit(pe, *u(2), 0)
                pe.wait_ge(a_ev, i * 4 + 2)
                pe_unit(pe, *u(3), 2, between=turn)

                def kv(n):
                    t, r = n // 2, slice(64 * (n % 2), 64 * (n % 2) + 64)
                    if n % 2 == 0:
                        pe.wait_ge(tok_lo_s, i * 8 + (t + 1))
                    if n >= 2:
                        pe.wait_ge(st_new, i * NCH + (n - 1))
                    for p, (k_, v_) in enumerate(((tok_hi, tok_hi), (tok_hi, tok_lo), (tok_lo, tok_hi))):
                        last = pe.matmul(ps(4 + n % 2, 0, GLA_DV), k_[r, t, 0:P], v_[r, t, P:384],
                                         start=(p == 0), stop=(p == 2))
                    last.then_inc(kv_sum, 1)

                def read(m):
                    if m == 0:
                        pe.wait_ge(q_lo_s, i + 1)
                        pe.wait_ge(tok_lo_s, i * 8 + 8)
                    pe.wait_ge(st_lo_s, i * NCH + (m + 1))
                    if m >= 2:
                        pe.wait_ge(o_ev, i * NCH + (m - 1))
                    for p, (s_, q_) in enumerate(((st_hi, g_hi), (st_hi, g_lo), (st_lo, g_hi))):
                        last = pe.matmul(ps(6 + m % 2, 0, GLA_DV), q_[:, blk(m // 2)], s_[m % 2][:],
                                         start=(p == 0), stop=(p == 2))
                    last.then_inc(o_sum, 1)

                def scan(n):
                    kv(n)
                    if n:
                        read(n - 1)
                pe_unit(pe, *u(4), 0, between=scan)
                pe.wait_ge(q_lo_s, i + 1)
                read(NCH - 1)
                pe_unit(pe, *u(5), 2)
                pe.wait_ge(o_scaled, i + 1)
                for dt in range(2):
                    for t in range(8):
                        last = pe.transpose(ps(4 + 2 * dt + t // 4, (t % 4) * P, (t % 4 + 1) * P),
                                            o_tok[:, t, blk(dt)], ident[:])
                    last.then_inc(o_turned, 1)

        def act_gla(act):
            act_w(act, U_GLR % 2, U_GLR + 2)
            act.wait_ge(unit_done, U_GLR + 1)
            act.activation(glr[:], pair(4, 0, GLA_RANK), ACT.Copy).then_inc(a_ev, 1)
            with act.Fori(0, GLA_HEADS) as i:
                AC.enter(i, 2 + 1)

                def ahead(d):
                    act_w(act, (U_GLA + d) % 2, i * GLA_PER_HEAD + (U_GLA + d + 2))
                    act_ada_load(act, (ADA_FIRST + d + 1) % 2, i * GLA_PER_HEAD + (ADA_FIRST + d + 1))

                def done(d):
                    act.wait_ge(unit_done, i * GLA_PER_HEAD + (U_GLA + d + 1))
                act.wait_ge(gate_sum, i + 1)
                AC.link(act.activation(g_t1[:], pair(4), ACT.Abs, bias=gla_b[:]))
                AC.link(act.activation(g_t1[:], g_t1[:], ACT.Exp, scale=-1.0))
                act.activation(g_t1[:], g_t1[:], ACT.Ln, bias=ones[:, 0:1]).then_inc(gate_ln, 1)
                act.wait_ge(gate_cum, i + 1)
                act.activation(g_t2[:], g_t2[:], ACT.Exp, scale=1.0 / GLA_TEMP).then_inc(decay_ready, 1)
                act.activation(dec[:], g_t1[:].rearrange("p (n l) -> p n l", l=CHUNK)[:, :, CHUNK - 1],
                               ACT.Exp, scale=1.0 / GLA_TEMP).then_inc(decay_ready, 1)
                ahead(0)
                for dt in range(2):
                    done(1 + dt)
                    act.activation(g_v[:, dt, :], pair(2 - 2 * dt), ACT.Copy).then_inc(a_ev, 1)
                    ahead(1 + dt)
                for t in range(8):
                    act.wait_ge(tok_sum, i * 8 + (t + 1))
                    act.activation(tok_hi[:, t, :], ps(6 + t % 2, 0, 384), ACT.Copy).then_inc(tok_hi_s, 1)
                done(3)
                act.activation(g_hi[:], pair(2), ACT.Copy, scale=QSCALE).then_inc(q_hi_s, 1)
                ahead(3)
                def leave(m):
                    rows = slice(64 * (m % 2), 64 * (m % 2) + 64)
                    act.wait_ge(o_sum, i * NCH + (m + 1))
                    act.activation(o_tok[rows, m // 2, :], ps(6 + m % 2, 0, GLA_DV, rows.start, rows.stop),
                                   ACT.Copy).then_inc(o_ev, 1)
                for n in range(NCH):
                    act.wait_ge(st_new, i * NCH + (n + 1))
                    if n >= 2:
                        act.wait_ge(o_sum, i * NCH + (n - 1))
                    act.activation(st_hi[n % 2][:], st[n % 2][:], ACT.Copy).then_inc(st_hi_s, 1)
                    if n >= 2:
                        leave(n - 2)
                leave(NCH - 2)
                leave(NCH - 1)
                act.wait_ge(o_ev, i * NCH + NCH)
                act.activation(o_sq[:], o_tok[:], ACT.Square).then_inc(NG.squared, 1)
                done(4)
                act.activation(g_r[:, 0, :], pair(0), ACT.Silu).then_inc(a_ev, 1)
                act.wait_ge(NG.summed, i + 1)
                AC.link(act.activation(mx[:], mx[:], ACT.Ln, bias=eps[:], scale=1.0 / GLA_DV))
                act.activation(mx[:], mx[:], ACT.Exp, scale=-0.5).then_inc(NG.rstd, 1)
                ahead(4)
                done(5)
                act.activation(g_r[:, 1, :], pair(2), ACT.Silu).then_inc(a_ev, 1)
                ahead(5)
                AC.leave(GLA_HEADS)
            for k in range(KT):
                act.wait_ge(o_gated, k + 3)
                act.activation(a_hi[:, k, :], o_all[:, k, :], ACT.Copy).then_inc(o_hi_s, 1)
            act.wait_ge(o_lo_s, KT)
            act.dma_start(x[:], x_in).then_inc(x_loaded[1], 16)

        def dve_gla(dve):
            dve.sem_inc(o_gated, 2)
            with dve.Fori(0, GLA_HEADS) as i:
                V.enter(i, 1 + 1 + NCH + 1 + GLA_PER_HEAD)

                def ada_col(d):
                    dve_ada_ring(dve, V, (ADA_FIRST + d) % 2, i * GLA_PER_HEAD + (ADA_FIRST + d))
                dve.tensor_copy(gate_w[:], gate_all[:, ds(i * GLA_DK, GLA_DK)])
                dve.tensor_copy(gla_b[:], col[:, ds(i + C_BGATE, 1)]).then_inc(gw_ready, 1)
                dve.wait_ge(gw_ready, i + 1)
                dve.wait_ge(gate_ln, i + 1)
                V.link(dve.tensor_scalar(g_t2[:], pair(4), gla_b[:], 0.0, ALU.add, ALU.min))
                V.link(dve.tensor_tensor(g_t2[:], g_t2[:], g_t1[:], ALU.subtract))
                for n in range(NCH):
                    cs = slice(n * CHUNK, (n + 1) * CHUNK)
                    last = V.mark(dve.tensor_tensor_scan(out=g_t1[:, cs], data0=ones[:, 0:CHUNK], data1=g_t2[:, cs],
                                                         initial=0.0, op0=ALU.mult, op1=ALU.add))
                dve.wait_ge(dve_s, last)
                cum = g_t1[:].rearrange("p (n l) -> p n l", l=CHUNK)
                dve.tensor_tensor(g_t2[:].rearrange("p (n l) -> p n l", l=CHUNK),
                                  cum[:, :, CHUNK - 1:CHUNK].to_broadcast([P, NCH, CHUNK]), cum,
                                  ALU.subtract).then_inc(gate_cum, 1)
                ada_col(0)
                dve.wait_ge(unit_done, i * GLA_PER_HEAD + (U_GLA + 1))
                dve.wait_ge(decay_ready, i * 2 + 1)
                dve.tensor_tensor(g_k[:], pair(0), g_t2[:], ALU.mult).then_inc(kend, 1)
                for d in range(1, 4):
                    ada_col(d)
                for t in range(8):
                    dve.wait_ge(tok_hi_s, i * 8 + (t + 1))
                    dve.tensor_tensor(tok_lo[:, t, :], ps(6 + t % 2, 0, 384), f(tok_hi[:, t, :]),
                                      ALU.subtract).then_inc(tok_lo_s, 1)
                V.link(dve.memset(st[1][:], 0.0))
                dve.wait_ge(q_hi_s, i + 1)
                dve.scalar_tensor_tensor(out=g_lo[:], in0=pair(2), scalar=QSCALE, in1=f(g_hi[:]), op0=ALU.mult,
                                         op1=ALU.subtract).then_inc(q_lo_s, 1)

                def state(n):
                    dve.wait_ge(kv_sum, i * NCH + (n + 1))
                    if n == 0:
                        dve.wait_ge(decay_ready, i * 2 + 2)
                    else:
                        dve.wait_ge(st_new, i * NCH + n)
                    dve.scalar_tensor_tensor(out=st[n % 2][:], in0=st[(n + 1) % 2][:], scalar=dec[:, n:n + 1],
                                             in1=ps(4 + n % 2, 0, GLA_DV), op0=ALU.mult,
                                             op1=ALU.add).then_inc(st_new, 1)
                state(0)
                for n in range(NCH):
                    dve.wait_ge(st_hi_s, i * NCH + (n + 1))
                    if n >= 2:
                        dve.wait_ge(o_sum, i * NCH + (n - 1))
                    dve.tensor_tensor(st_lo[n % 2][:], st[n % 2][:], f(st_hi[n % 2][:]), ALU.subtract).then_inc(st_lo_s, 1)
                    if n + 1 < NCH:
                        state(n + 1)
                dve.wait_ge(NG.squared, i + 1)
                dve.tensor_reduce(out=mx[:], in_=o_sq[:], axis=AX, op=ALU.add).then_inc(NG.summed, 1)
                ada_col(4)
                dve.wait_ge(NG.rstd, i + 1)
                dve.tensor_tensor(o_tok[:], o_tok[:], mx[:].rearrange("p (t o) -> p t o", o=1).to_broadcast([P, 8, GLA_DV]),
                                  ALU.mult).then_inc(o_scaled, 1)
                ada_col(5)
                for dt in range(2):
                    dve.wait_ge(a_ev, i * 4 + (4 + dt))
                    dve.wait_ge(o_turned, i * 2 + (dt + 1))
                    dve.scalar_tensor_tensor(out=o_all[:, ds(i * 2 + dt, 1), :].rearrange("p a n -> p (a n)"),
                                             in0=pair(4 + 2 * dt), scalar=col[:, C_HEADG + dt:C_HEADG + dt + 1],
                                             in1=g_r[:, dt, :], op0=ALU.mult, op1=ALU.mult).then_inc(o_gated, 1)
                V.leave(GLA_HEADS)
            for k in range(KT):
                dve.wait_ge(o_hi_s, k + 1)
                dve.tensor_tensor(a_lo[:, k, :], o_all[:, k, :], f(a_hi[:, k, :]), ALU.subtract).then_inc(o_lo_s, 1)

        NQ, NKV = Norm("mla_q"), Norm("mla_kv")
        ang_s, sin_s, tables = sem("rope_angles"), sem("rope_sines"), sem("rope_tables")
        pos_loaded, ident_s = sem("positions_loaded"), sem("identity_rounded")
        c_ev, kr_s, c_val, c_hi_s, c_lo_s = (sem(f"mla_{s}") for s in ("c_evacuated", "k_rope", "c_value", "c_hi", "c_lo"))
        fixed_s, pad_s = sem("mla_shared_rows"), sem("mla_pads")
        sc_sum, p_exp, p_hi_s, p_lo_s, pv_done = (sem(f"mla_{s}") for s in (
            "scores", "p_exp", "p_hi", "p_lo", "pv_done"))
        prep, qf_s, rp_s, qhi_s, qlo_s, khi_s, klo_s, vf_s = (sem(f"mla_{s}") for s in (
            "projected", "q_copied", "q_roped", "q_hi", "q_lo", "k_hi", "k_lo", "v_copied"))
        vt_sum, vhi_s, vlo_s, mx_sum, mx_used, mx_s, row_sum, row_s = (sem(f"mla_{s}") for s in (
            "v_transposed", "v_hi", "v_lo", "max_scores", "max_read", "max", "max_rows", "max_row_set"))
        sums_back = sem("mla_sums_back")
        o_out, sums_kept = sem("mla_o_evacuated"), [sem(f"mla_sums_kept{j}") for j in range(2)]
        sel_s, rec_s, bc_sum, on_s, oh_s, ol_s = (sem(f"mla_{s}") for s in (
            "selector", "reciprocals", "reciprocals_spread", "o_normed", "o_hi", "o_lo"))
        SM = (NOPE + ROPE) ** -0.5
        R0, R1, R2 = NOPE, NOPE + ROPE, NOPE + 2 * ROPE
        DT = NOPE + ROPE
        QI = [(half, k) for half in range(2) for k in range(QT)]
        KI = [(half, k) for half in range(2) for k in range(QT, QT + KVT)]
        BLOCKS = [(half, j, max(P * j, HALF * half), HALF * (half + 1)) for half in range(2) for j in range(4 * half + 4)]
        NB = len(BLOCKS)

        def pe_mla_in(pe):
            for m in range(MLA_IN_UNITS):
                u = U_MLA_IN + m
                if m == 0:
                    pe_first(pe, 2, u, (0, 2))
                if m >= 2:
                    pe.wait_ge(c_ev, m - 1)
                    pe_unit(pe, u % 2, u, 2 * (m % 2))
                if m == MLA_IN_UNITS - 2:
                    pe_sums(pe, NQ, QI, c_sq, 4, 0, QT - 1)
            pe_sums(pe, NKV, KI, c_sq, 6, QT, QT + KVT - 1)

        def act_spill(act):
            act.dma_start(pos_i[R0:R1], pos_in).then_inc(pos_loaded, 16)
            act.dma_start(x_mid, x[:]).then_inc(x_spilled, 16)

        def act_mla_in(act):
            PRE.wait_lo(act, 2, 1)
            act.wait_ge(ada_done, N_ADA)
            act.activation(ident_r[:], ident[:], ACT.Copy).then_inc(ident_s, 1)
            act.wait_ge(ang_s, 1)
            act.activation(sin_t[R0:R1], ang[R0:R1], ACT.Sin).then_inc(sin_s, 1)
            AC.link(act.activation(turns[R0:R1], ang[R0:R1], ACT.Abs))
            act.activation(cos_t[R0:R1], turns[R0:R1], ACT.Sin, bias=halfpi[R0:R1], scale=-1.0).then_inc(sin_s, 1)

            def high(m0, m1):
                for m in range(m0, m1):
                    act.wait_ge(c_val, m + 1)
                    act.activation(c_hi[:, m, :], c_f[:, m, :], ACT.Copy).then_inc(c_hi_s, 1)
            for m in range(MLA_IN_UNITS):
                u = U_MLA_IN + m
                act_w(act, u % 2, u + 2)
                if m == 0:
                    act.wait_ge(x_spilled, 16)
                act.wait_ge(unit_done, u + 1)
                if m < MLA_IN_UNITS - 1:
                    act.activation(c_f[:, m, :], pair(2 * (m % 2)), ACT.Copy).then_inc(c_ev, 1)
                if m == MLA_IN_UNITS - 3:
                    act.wait_ge(c_ev, QT)
                    act_squares(act, NQ, c_f, QI, c_sq)
                if m == MLA_IN_UNITS - 2:
                    for half in range(2):
                        act_rstd(act, NQ.summed, NQ.rstd, half, 4 + half, rstd_q, Q_RANK, QT * (half + 1))
                    act.wait_ge(c_ev, MLA_IN_UNITS - 1)
                    act.wait_ge(NQ.summed, len(QI))
                    act_squares(act, NKV, c_f, KI, c_sq)
                    high(0, QT)
            for half in range(2):
                act_rstd(act, NKV.summed, NKV.rstd, half, 6 + half, rstd_kv, KV_RANK, KVT * (half + 1))
            high(QT, QT + KVT)
            act.wait_ge(kr_s, 1)
            for j in range(2):
                act.activation(k_hi[j][R0:R1], krope[R0:R1], ACT.Copy).then_inc(fixed_s, 1)

        def dve_mla_in(dve):
            dve.wait_ge(pos_loaded, 16)
            F, G = slice(R0, R1), col[R0:R1, C_FREQ:C_FREQ + 1]
            V.link(dve.tensor_copy(ang[F], pos_i[F]))
            V.link(dve.tensor_scalar(ang[F], ang[F], G, None, ALU.mult))
            V.link(dve.tensor_scalar(turns[F], ang[F], 0.15915494309189535, ROUND, ALU.mult, ALU.add))
            V.link(dve.tensor_scalar(turns[F], turns[F], ROUND, None, ALU.subtract))
            for c in TWO_PI:
                V.link(dve.scalar_tensor_tensor(out=ang[F], in0=turns[F], scalar=-c, in1=ang[F], op0=ALU.mult, op1=ALU.add))
            dve.tensor_scalar(ang[F], ang[F], PI, -PI, ALU.min, ALU.max).then_inc(ang_s, 1)
            dve.wait_ge(sin_s, 2)
            dve.tensor_scalar(sin_t[F], sin_t[F], col[F, C_SIGN:C_SIGN + 1], None, ALU.mult).then_inc(tables, 1)
            dve.wait_ge(x_spilled, 16)

            def scaled(m0, m1, r, nm):
                dve.wait_ge(nm.rstd, 2)
                for m in range(m0, m1):
                    dve.scalar_tensor_tensor(out=c_f[:, m, :], in0=c_f[:, m, :], scalar=col[:, C_QG + m:C_QG + m + 1],
                                             in1=r[:], op0=ALU.mult, op1=ALU.mult).then_inc(c_val, 1)
                for m in range(m0, m1):
                    dve.wait_ge(c_hi_s, m + 1)
                    dve.tensor_tensor(c_lo[:, m, :], c_f[:, m, :], f(c_hi[:, m, :]), ALU.subtract).then_inc(c_lo_s, 1)
            scaled(0, QT, rstd_q, NQ)
            dve.wait_ge(tables, 1)
            dve.wait_ge(unit_done, U_MLA_IN + MLA_IN_UNITS)
            b = 2 * ((MLA_IN_UNITS - 1) % 2)
            V.link(dve.tensor_tensor(krope[F], pair(b, R0, R1), cos_t[F], ALU.mult))
            for half in range(2):
                V.link(dve.tensor_tensor(rope_t[F], ps(b + half, r0=R1, r1=R2), sin_t[F, hs(half)], ALU.mult))
                last = V.mark(dve.tensor_tensor(krope[F, hs(half)], krope[F, hs(half)], rope_t[F], ALU.add))
                dve.wait_ge(dve_s, last)
            dve.sem_inc(kr_s, 1)
            scaled(QT, QT + KVT, rstd_kv, NKV)
            for j in range(2):
                dve.wait_ge(fixed_s, j + 1)
                dve.tensor_tensor(k_lo[j][F], krope[F], f(k_hi[j][F]), ALU.subtract).then_inc(kr_s, 1)

        def pool_pads(pool):
            pool.wait_ge(unit_done, U_MLA_IN + MLA_IN_UNITS)
            pool.wait_ge(lo_ready, U_MLA + 2)
            n = 0
            for j in range(2):
                c = MLA_V * (1 - j)
                for t, v in ((k_hi[j][DT:DT + 1], -1.0), (k_lo[j][DT:DT + 1], 0.0), (q_lo[j][DT:DT + 1], 0.0),
                             (v_lo[j][:, :, c:c + 64], 0.0), (v_hi[j][:, :, c + 1:c + 64], 0.0),
                             (v_hi[j][:, :, c:c + 1], 1.0)):
                    wait(pool, pad_s, n)
                    pool.memset(f(t), v).then_inc(pad_s, 1)
                    n += 1
            pool.wait_ge(pad_s, n)

        def pe_prep(pe, s, h, j, i):
            def c(k, d=0):
                return plus(i, 2 * k, k * h + d)
            if s < 4:
                kind, half = s // 2, s % 2
                if s == 0:
                    pe.wait_ge(lo_ready, plus(i, 2, U_MLA + h + 1))
                if kind == 0:
                    wait(pe, mx_used, c(8))
                else:
                    wait(pe, row_s, c(1))
                tiles = range(QT) if kind == 0 else range(QT, QT + KVT)
                for t in tiles:
                    for p, (w, a) in enumerate(((w_hi, c_hi), (w_hi, c_lo), (w_lo, c_hi))):
                        last = pe.matmul(ps(4 + s), w[(U_MLA + j) % 2][:, blk(t)], a[:, t, hs(half)],
                                         start=(t == tiles[0] and p == 0), stop=(t == tiles[-1] and p == 2))
                last.then_inc(prep if s < 3 else unit_done, 1)
            elif s == 5:
                for t in range(8):
                    last = pe.transpose(ps(4, 64 * t, 64 * t + 64), v_f[64:128, blk(t)], ident[64:128, 64:128])
                last.then_inc(vt_sum, 1)
            elif 7 <= s < 11:
                if s == 7:
                    pe.wait_ge(qhi_s, c(2, 2))
                    pe.wait_ge(klo_s, c(2, 2))
                    pe.wait_ge(fixed_s, 2)
                for t in (2 * (s - 7), 2 * (s - 7) + 1):
                    if t == 1:
                        pe.wait_ge(vlo_s, c(1, 1))
                    if t >= 2:
                        pe.wait_ge(mx_used, c(8, t - 1))
                    b = 6 - 2 * (t % 2)
                    for k0 in range(0, P * (t + 1), HALF):
                        k1 = min(k0 + HALF, P * (t + 1))
                        last = pe.matmul(ps(b + k0 // HALF, 0, k1 - k0), q_hi[j][0:R1, blk(t)], k_hi[j][0:R1, k0:k1],
                                         start=True, stop=True)
                    last.then_inc(mx_sum, 1)
            elif s == 12:
                pe.wait_ge(mx_s, c(1, 1))
                for t in range(8):
                    last = pe.matmul(ps(6 + t // 4, P * (t % 4), P * (t % 4) + P),
                                     mx_r[:, t:t + 1].to_broadcast([P, P]), ident_r[:], start=True, stop=True)
                last.then_inc(row_sum, 1)

        def projected(eng, s, h, i):
            if s < 3:
                eng.wait_ge(prep, plus(i, 6, 3 * h + s + 1))
            else:
                eng.wait_ge(unit_done, plus(i, 2, U_MLA + h + 1))

        def act_prep(act, s, h, j, i):
            def c(k, d=0):
                return plus(i, 2 * k, k * h + d)
            if s < 4:
                kind, half = s // 2, s % 2
                projected(act, s, h, i)
                if kind == 0:
                    wait(act, qlo_s, c(2, half - 1))
                    act.activation(q_f[0:R0, hs(half)], ps(4 + s, r1=R0), ACT.Copy).then_inc(qf_s, 1)
                else:
                    act.activation(k_hi[j][0:R0, hs(half)], ps(4 + s, r1=R0), ACT.Copy).then_inc(khi_s, 1)
                    act.activation(v_f[R0:P, hs(half)], ps(4 + s, r0=R0), ACT.Copy).then_inc(vf_s, 1)
            elif s == 4:
                for half in range(2):
                    act.wait_ge(rp_s, c(2, half + 1))
                    act.wait_ge(qf_s, c(2, half + 1))
                    act.activation(q_hi[j][0:R1, hs(half)], q_f[0:R1, hs(half)], ACT.Copy).then_inc(qhi_s, 1)
                act_w(act, (U_MLA + j) % 2, plus(i, 2, U_MLA + h + 2))
            elif s == 5:
                act.wait_ge(vt_sum, c(1, 1))
                act.activation(v_hi[j][:, :, 64 * j:64 * j + 64], ps(4).rearrange("p (t c) -> p t c", c=64),
                               ACT.Copy).then_inc(vhi_s, 1)
            elif s == 12:
                act.wait_ge(row_sum, c(1, 1))
                act.activation(q_hi[j][DT:DT + 1], pair(6, DT, DT + 1), ACT.Copy).then_inc(row_s, 1)

        def dve_prep(dve, s, h, j, i):
            def c(k, d=0):
                return plus(i, 2 * k, k * h + d)
            if s < 2:
                projected(dve, s, h, i)
                V.link(dve.tensor_tensor(q_f[R0:R1, hs(s)], ps(4 + s, r0=R0, r1=R1), cos_t[R0:R1, hs(s)], ALU.mult))
                V.link(dve.tensor_tensor(rope_t[R0:R1], ps(4 + s, r0=R1, r1=R2), sin_t[R0:R1, hs(s)], ALU.mult))
                dve.tensor_tensor(q_f[R0:R1, hs(s)], q_f[R0:R1, hs(s)], rope_t[R0:R1], ALU.add).then_inc(rp_s, 1)
                dve.wait_ge(rp_s, c(2, s + 1))
            elif s < 4:
                half = s % 2
                dve.wait_ge(khi_s, c(2, half + 1))
                dve.tensor_tensor(k_lo[j][0:R0, hs(half)], ps(4 + s, r1=R0), f(k_hi[j][0:R0, hs(half)]),
                                  ALU.subtract).then_inc(klo_s, 1)
            elif s == 4:
                for half in range(2):
                    dve.wait_ge(qhi_s, c(2, half + 1))
                    dve.tensor_tensor(q_lo[j][0:R1, hs(half)], q_f[0:R1, hs(half)], f(q_hi[j][0:R1, hs(half)]),
                                      ALU.subtract).then_inc(qlo_s, 1)
            elif s == 5:
                dve.wait_ge(vhi_s, c(1, 1))
                vs = slice(64 * j, 64 * j + 64)
                dve.tensor_tensor(v_lo[j][:, :, vs], ps(4).rearrange("p (t c) -> p t c", c=64), f(v_hi[j][:, :, vs]),
                                  ALU.subtract).then_inc(vlo_s, 1)
            elif 7 <= s < 11:
                for t in (2 * (s - 7), 2 * (s - 7) + 1):
                    dve.wait_ge(mx_sum, c(8, t + 1))
                    src = psum[:, 6 - 2 * (t % 2):8 - 2 * (t % 2), :].rearrange("p a b -> p (a b)")
                    n = P * t + CHUNK
                    V.mark(dve.reduce_max(mx[:, t:t + 1], src[:, 0:n], axis=AX))
                    dve.reduce_max(mx2[64:128, t:t + 1], src[64:128, n:n + CHUNK], axis=AX).then_inc(mx_used, 1)
                if s == 10:
                    dve.wait_ge(mx_used, c(8, 8))
                    dve.wait_ge(dve_s, V.at())
                    V.link(dve.tensor_tensor(mx[64:128], mx[64:128], mx2[64:128], ALU.max))
                    wait(dve, row_s, c(1))
                    dve.tensor_copy(mx_r[:], mx[:]).then_inc(mx_s, 1)

        PREP_V = 2 * 2 + 8 + 1

        def pe_v_ready(pe, h, i):
            for s_ in (vf_s, qf_s, rp_s):
                pe.wait_ge(s_, plus(i, 4, 2 * h + 2))

        def pe_head(pe, h, j, i, follow):
            def c(k, d=0):
                return plus(i, 2 * k, k * h + d)
            pe.wait_ge(row_s, c(1, 1))
            pe.wait_ge(qlo_s, c(2, 2))
            if h == 0 and i is not None:
                pe.wait_ge(pad_s, 12)
                pe.wait_ge(kr_s, 3)
            for s in range(NB + 3):
                if follow and s == 5:
                    pe_v_ready(pe, h + 1, i)
                if s < NB:
                    half, t, q0, q1 = BLOCKS[s]
                    pe.wait_ge(p_exp, c(NB, s + 1))
                    for p, (k_, q_) in enumerate(((k_hi, q_hi), (k_hi, q_lo), (k_lo, q_hi))):
                        last = pe.matmul(ps(2 + s % 2, 0, q1 - q0), k_[j][0:DT + 1, blk(t)], q_[j][0:DT + 1, q0:q1],
                                         start=(p == 0), stop=(p == 2))
                    last.then_inc(sc_sum, 1)
                if follow:
                    pe_prep(pe, s, h + 1, 1 - j, i)
                if s >= 3:
                    m = s - 3
                    half, t, q0, q1 = BLOCKS[m]
                    pe.wait_ge(p_lo_s, c(NB, m + 5))
                    if t == 0:
                        pe.wait_ge(o_out, c(2, half + 1))
                    b0 = q0 - HALF * half
                    for p, (v_, p_) in enumerate(((v_hi, p_hi), (v_hi, p_lo), (v_lo, p_hi))):
                        last = pe.matmul(ps(half, b0, HALF), v_[j][:, t, :], p_[m % 4][:, 0:q1 - q0],
                                         start=(t == 0 and p == 0), stop=(t == 4 * half + 3 and p == 2))
                    last.then_inc(pv_done, 1)

        def act_head(act, h, j, i, follow):
            def c(k, d=0):
                return plus(i, 2 * k, k * h + d)
            rows = slice(64 * j, 64 * j + 64)
            srow = 64 * (1 - j)

            def leave(half):
                act.wait_ge(pv_done, c(NB, (4 if half == 0 else NB) + 4))
                act.wait_ge(consts, 5)
                act.activation(o_un[rows, ds(plus(i, 1, h // 2), 1), hs(half)].rearrange("p a n -> p (a n)"),
                               ps(half, r0=64 * j, r1=64 * j + 64), ACT.Copy)
                act.wait_ge(sums_kept[j], plus(i, 16, 8 * (h - j) + 16))
                act.activation(sums[srow:srow + 1, hs(half)], ps(half, r0=srow, r1=srow + 1), ACT.Copy).then_inc(o_out, 1)
            for s in range(NB + 3):
                if s < NB:
                    half, t, q0, q1 = BLOCKS[s]
                    act.wait_ge(sc_sum, c(NB, s + 1))
                    act.wait_ge(p_lo_s, c(NB, s + 1))
                    act.activation(p_f[s % 4][:, 0:q1 - q0], ps(2 + s % 2, 0, q1 - q0), ACT.Exp,
                                   scale=SM).then_inc(p_exp, 1)
                if follow:
                    act_prep(act, s, h + 1, 1 - j, i)
                if s == 7:
                    leave(0)
            leave(1)
            act.wait_ge(o_out, c(2, 4))
            act.dma_start(sums_dram[ds(plus(i, 2, h), 1), :], sums[srow:srow + 1, :]).then_inc(sums_kept[j], 16)

        def dve_head(dve, h, j, i, follow):
            for s in range(NB + 3):
                if s < NB:
                    half, t, q0, q1 = BLOCKS[s]
                    dve.wait_ge(p_exp, plus(i, 2 * NB, NB * h + s + 3))
                    if q0 == P * t:
                        V.link(dve.memset(p_f[s % 4][64:128, 0:CHUNK], 0.0))
                    dve.wait_ge(pv_done, plus(i, 2 * NB, NB * h + s + 1))
                    dve.tensor_copy(p_hi[s % 4][:, 0:q1 - q0], p_f[s % 4][:, 0:q1 - q0]).then_inc(p_hi_s, 1)
                if follow:
                    dve_prep(dve, s, h + 1, 1 - j, i)

        def pool_head(pool, h, j, i, follow):
            for s in range(NB):
                half, t, q0, q1 = BLOCKS[s]
                pool.wait_ge(p_hi_s, plus(i, 2 * NB, NB * h + s + 1))
                pool.tensor_tensor(p_lo[s % 4][:, 0:q1 - q0], p_f[s % 4][:, 0:q1 - q0], f(p_hi[s % 4][:, 0:q1 - q0]),
                                   ALU.subtract).then_inc(p_lo_s, 1)
                if follow and s == 6:
                    pool_w(pool, (U_MLA + 1 - j) % 2, plus(i, 2, U_MLA + h + 3))

        def mla_heads(eng, head, prep_step, steps=None):
            for s in range(NB + 1):
                if s == 5 and prep_step is pe_prep:
                    pe_v_ready(eng, 0, None)
                prep_step(eng, s, 0, 0, None)
            with eng.Fori(0, MLA_HEADS // 2 - 1) as i:
                if steps:
                    steps.enter(i, 2 * (8 + PREP_V))
                head(eng, 0, 0, i, True)
                head(eng, 1, 1, i, True)
                if steps:
                    steps.leave(MLA_HEADS // 2 - 1)
            head(eng, MLA_HEADS - 2, 0, None, True)
            head(eng, MLA_HEADS - 1, 1, None, False)

        def pool_prep(pool, s, h, j, i):
            if s == 4:
                pool_w(pool, (U_MLA + j) % 2, U_MLA + h + 2)

        def all_kept(eng):
            eng.wait_ge(sums_back, 16)

        def pe_mla_norm(pe):
            pe.wait_ge(sel_s, 3)
            pe.wait_ge(o_out, 2 * MLA_HEADS + 2)
            for m in range(KT):
                if m >= 4:
                    pe.wait_ge(on_s, m - 3)
                for half in range(2):
                    pe.wait_ge(rec_s, half + 1)
                    last = pe.matmul(ps(2 * (m % 4) + half), select[:, blk(m)], recip[:, hs(half)], start=True, stop=True)
                last.then_inc(bc_sum, 1)
            pe.wait_ge(on_s, KT)

        def dve_mla_norm(dve):
            all_kept(dve)
            for half in range(2):
                dve.reciprocal(recip[:, hs(half)], sums_all[:, hs(half)]).then_inc(rec_s, 1)
            for m in range(KT):
                dve.wait_ge(bc_sum, m + 1)
                dve.tensor_tensor(o_un[:, m, :], o_un[:, m, :], pair(2 * (m % 4)), ALU.mult).then_inc(on_s, 1)
                if m:
                    low(dve, m - 1)
            low(dve, KT - 1)

        def low(dve, m):
            dve.wait_ge(oh_s, m + 1)
            dve.tensor_tensor(a_lo[:, m, :], o_un[:, m, :], f(a_hi[:, m, :]), ALU.subtract).then_inc(ol_s, 1)

        def act_mla_norm(act):
            for j in range(2):
                act.wait_ge(sums_kept[j], 16 * MLA_HEADS // 2 + 16)
            act.dma_start(sums_all[:], sums_dram).then_inc(sums_back, 16)
            for m in range(KT):
                act.wait_ge(on_s, m + 1)
                act.activation(a_hi[:, m, :], o_un[:, m, :], ACT.Copy).then_inc(oh_s, 1)
            act.wait_ge(ol_s, KT)
            act.dma_start(x[:], x_mid).then_inc(x_loaded[2], 16)

        def pool_select(pool):
            all_kept(pool)
            pool.memset(select[:], 1.0).then_inc(sel_s, 1)
            pool.wait_ge(sel_s, 1)
            pool.affine_select(out=select[:], in_=select[:], compare_op=ALU.is_ge, fill=0.0, base=0,
                               pattern=[[1, S]], channel_multiplier=-MLA_V).then_inc(sel_s, 1)
            pool.wait_ge(sel_s, 2)
            pool.affine_select(out=select[:], in_=select[:], compare_op=ALU.is_ge, fill=0.0, base=MLA_V - 1,
                               pattern=[[-1, S]], channel_multiplier=MLA_V).then_inc(sel_s, 1)

        Y_DONE = [(out_free[0], KT + 2), (down_free[0], 8 * NFB + 2), (out_free[1], KT + 2), (down_free[1], 8 * NFB + 2)]

        with nc.Block() as block:
            @block.sync
            def _(sp):
                def load(j, u):
                    sp.dma_start(w_raw[j][:], units[ds(u, 1)].rearrange("a p n -> p (a n)")).then_inc(w_loaded[j], 16)
                sp.dma_start(x[:], x_in).then_inc(x_loaded[0], 16)
                sp.dma_start(col[:], cols).then_inc(par_in, 16)
                for u in range(2):
                    load(u, u)
                with sp.Fori(0, (UNITS - 2) // 2) as i:
                    for d in range(2):
                        sp.wait_ge(lo_ready, i * 2 + (d + 1))
                        load(d, i * 2 + (d + 2))
                for u in range(UNITS - (UNITS - 2) % 2, UNITS):
                    sp.wait_ge(lo_ready, u - 1)
                    load(u % 2, u)
                for half in range(2):
                    wait_share(sp, 3, KT * half + KT - 1, x_pool, x_dve)
                    wait_share(sp, 3, KT * half + KT - 2, x_pool, x_dve)
                    sp.dma_start(out[:, :, hs(half)], x[:, :, hs(half)]).then_inc(stored, 16)
                sp.wait_ge(stored, 32)

            @block.gpsimd
            def _(pool):
                pool.memset(ones[:], 1.0).then_inc(consts, 1)
                pool.memset(eps[:], EPS).then_inc(consts, 1)
                pool.memset(halfpi[:], 1.5707963267948966).then_inc(consts, 1)
                pool.memset(ident[:], 0.0).then_inc(consts, 1)
                pool.wait_ge(consts, 4)
                pool.affine_select(out=ident[:], in_=ident[:], compare_op=ALU.not_equal, fill=1.0, base=0,
                                   pattern=[[-1, P]], channel_multiplier=1).then_inc(consts, 1)
                for u in range(2):
                    pool_w(pool, u, u)
                for n in range(4):
                    pool.sem_inc(y_sq_added[n], 2)
                pool_pre(pool, 0)
                pool_w(pool, U_GLR % 2, U_GLR + 2)
                pool_units(pool, U_GLA, U_GLA_OUT - U_GLA)
                pool_out(pool, 0, U_GLA_OUT)

                def zero_y(n):
                    pool.wait_ge(step_made, EACH * (n + 1))
                    pool.memset(y[:], 0.0).then_inc(y_zeroed, 1)
                pool_step(pool, 0)
                pool_pre(pool, 1)
                zero_y(0)
                pool_mlp(pool, 0, U_MLP0)
                pool_step(pool, 1)
                pool_pre(pool, 2)
                pool_units(pool, U_MLA_IN, MLA_IN_UNITS)
                pool_pads(pool)
                pool.sem_inc(p_lo_s, 4)
                mla_heads(pool, pool_head, pool_prep)
                pool_select(pool)
                pool_out(pool, 1, U_MLA_OUT)
                pool_step(pool, 2)
                pool_pre(pool, 3)
                zero_y(2)
                pool_mlp(pool, 1, U_MLP1)
                pool_step(pool, 3)

            @block.scalar
            def _(act):
                nonlocal AC
                AC = Steps(act, act_s)
                act.dma_start(cond[:], cond_in).then_inc(cond_loaded, 16)
                act.wait_ge(cond_loaded, 16)
                act.activation(cond[:], cond[:], ACT.Silu).then_inc(cond_ready, 1)
                act.wait_ge(x_loaded[0], 16)
                for n in range(4):
                    part = slice(n * ADA_PART, (n + 1) * ADA_PART)
                    act.dma_start(ada_first[:, part, :], ada[part].rearrange("a p n -> p a n")).then_inc(ada_in[n], 16)
                act_ada_load(act, ADA_FIRST % 2, ADA_FIRST)
                for u in range(2):
                    act_w(act, u, u)
                act.wait_ge(consts, 5)
                act_bridge(act, None, False, 1, 4)
                PRE.wait_lo(act, 0, 1)
                act.dma_start(gate_all[:], gate_up).then_inc(gate_in, 16)
                act_gla(act)
                act_out(act, 0, U_GLA_OUT, True)
                act_bridge(act, 0, True, 2, 4)
                act_mlp(act, 0, U_MLP0, True)
                act_bridge(act, 1, True, 3, 0, act_spill)
                act_mla_in(act)
                act.sem_inc(p_exp, 2)
                act.sem_inc(o_out, 2)
                for j in range(2):
                    act.sem_inc(sums_kept[j], 16)
                mla_heads(act, act_head, act_prep)
                act_mla_norm(act)
                act_out(act, 1, U_MLA_OUT, False)
                act_bridge(act, 2, True, 4, 4)
                act_mlp(act, 1, U_MLP1, False)
                act_bridge(act, 3, True, 0, 0)

            @block.vector
            def _(dve):
                nonlocal V
                V = Steps(dve, dve_s)

                def fold(count, *which):
                    for n, what in which:
                        dve_fold(dve, n, what)
                    dve.wait_ge(folded, count)
                dve.wait_ge(par_in, 16)
                dve.wait_ge(cond_ready, 1)
                for a in range(ADA_FIRST):
                    if a % ADA_PART == 0:
                        dve.wait_ge(ada_in[a // ADA_PART], 16)
                    dve_ada(dve, V, a % 2, a, ada_first[:, a, :])
                dve.wait_ge(ada_done, ADA_FIRST)
                fold(1, (0, "scale"))
                dve.wait_ge(consts, 5)
                dve_bridge(dve, None, False, 1)
                dve.wait_ge(gate_in, 16)
                dve_gla(dve)
                dve_out_adas(dve)
                dve.wait_ge(ada_done, 6 * KT)
                fold(4, (0, "gate"), (1, "scale"), (1, "gate"))
                dve_bridge(dve, 0, True, 2)
                dve_mlp(dve, 0, U_MLP0, True)
                dve.wait_ge(ada_done, N_ADA)
                fold(8, (2, "scale"), (2, "gate"), (3, "scale"), (3, "gate"))
                dve_bridge(dve, 1, True, 3)
                dve_mla_in(dve)
                mla_heads(dve, dve_head, dve_prep, V)
                dve_mla_norm(dve)
                dve_bridge(dve, 2, True, 4)
                dve_mlp(dve, 1, U_MLP1, False)
                dve_bridge(dve, 3, True, 0)

            @block.tensor
            def _(pe):
                pe.wait_ge(consts, 5)
                pe_bridge(pe, None, False, 1, 4)
                pe_gla(pe)
                pe_out(pe, 0, U_GLA_OUT, o_lo_s)
                pe_bridge(pe, 0, True, 2, 4)
                pe_mlp(pe, 0, U_MLP0)
                pe_bridge(pe, 1, True, 3, 0)
                pe_mla_in(pe)
                pe.wait_ge(c_lo_s, QT + KVT)
                pe.wait_ge(ident_s, 1)
                pe.sem_inc(pv_done, 4)
                mla_heads(pe, pe_head, pe_prep)
                pe_mla_norm(pe)
                pe_out(pe, 1, U_MLA_OUT, ol_s)
                pe_bridge(pe, 2, True, 4, 4)
                pe_mlp(pe, 1, U_MLP1)
                pe_bridge(pe, 3, True, 0, 0)


def kernel(**inputs):
    import numpy as np
    import concourse.bacc as bacc
    from concourse.bass_utils import run_bass_kernel_spmd as run

    g = {k: np.asarray(v) for k, v in inputs.items()}

    def tiles(w):
        k, m = w.shape
        return w.reshape(k // P, P, m // P, P).transpose(2, 1, 0, 3).reshape(m // P, P, k)

    def padded(w, n):
        return np.concatenate([w, np.zeros((w.shape[0], n - w.shape[1]), w.dtype)], axis=1)

    def mlp(layer):
        up = tiles(g["mlp_w_up"][layer]).reshape(NFB, 2, P, 1024)
        down = g["mlp_w_down"][layer].reshape(NFB, 2, P, 2, 4, P).transpose(0, 3, 2, 4, 1, 5).reshape(NFB, 2, P, 1024)
        order = [up[0]]
        for b in range(1, NFB):
            order += [up[b], down[b - 1]]
        return np.concatenate(order + [down[NFB - 1]])

    w = g["gla_w_in"][0]
    kw, vw = GLA_HEADS * GLA_DK, GLA_HEADS * GLA_DV
    wq, wk, wv, wr, wg = np.split(w, [kw, 2 * kw, 2 * kw + vw, 2 * kw + 2 * vw], axis=1)
    q, k, v, r = tiles(wq), tiles(wk), tiles(wv), tiles(wr)
    parts = [tiles(padded(wg, P))]
    for h in range(GLA_HEADS):
        parts += [k[h:h + 1], v[2 * h:2 * h + 2], q[h:h + 1], r[2 * h:2 * h + 2]]
    parts += [tiles(g["gla_w_out"][0]), mlp(0)]
    w = g["mla_w_in"][0]
    half = ROPE // 2
    kr = w[:, Q_RANK + KV_RANK:]
    zero = np.zeros((D, NOPE), w.dtype)
    parts += [tiles(w[:, :Q_RANK + KV_RANK]), tiles(np.concatenate([zero, kr, kr[:, half:], kr[:, :half]], axis=1))]
    wq = g["mla_w_uq"][0].reshape(QT, P, MLA_HEADS, NOPE + ROPE)
    wq = np.concatenate([wq, wq[..., NOPE + half:], wq[..., NOPE:NOPE + half]], axis=-1)
    wkv = g["mla_w_ukv"][0].reshape(KVT, P, MLA_HEADS, NOPE + MLA_V)
    heads = np.concatenate([wq, wkv, np.zeros((KT - QT - KVT, P, MLA_HEADS, P), wq.dtype)], axis=0)
    parts += [heads.transpose(2, 1, 0, 3).reshape(MLA_HEADS, P, 1024), tiles(g["mla_w_out"][0]), mlp(1)]
    units = np.ascontiguousarray(np.concatenate(parts))
    assert units.shape == (UNITS, P, 1024)

    def columns(v):
        return v.reshape(-1, P).T
    freq = (np.float32(THETA) ** (-np.arange(half, dtype=np.float32) / half)).astype(np.float32)
    sign = np.repeat(np.array([-1.0, 1.0], np.float32), half)
    place = np.zeros((P, 2), np.float32)
    place[NOPE:NOPE + ROPE, 0] = np.tile(freq, 2)
    place[NOPE:NOPE + ROPE, 1] = sign
    cols = np.ascontiguousarray(np.concatenate([
        columns(g["ada_b"]), columns(g["norm_pre_g"]), columns(g["norm_post_g"]), columns(g["gla_b_gate"]),
        columns(g["gla_head_g"]), columns(g["mla_q_norm_g"]), columns(g["mla_kv_norm_g"]), place], axis=1))
    arrays = {
        "x_in": np.ascontiguousarray(g["x"][0].T.reshape(KT, P, S).transpose(1, 0, 2)),
        "units": units,
        "ada": np.ascontiguousarray(g["ada_w"].transpose(0, 2, 1).reshape(N_ADA, P, D)),
        "cols": cols,
        "cond_in": np.ascontiguousarray(np.broadcast_to(g["c"], (P, D))),
        "gate_up": np.ascontiguousarray(g["gla_w_gate_up"][0]),
        "pos_in": np.ascontiguousarray(np.broadcast_to(g["positions"][0], (ROPE, S))),
    }
    nc = bacc.Bacc("TRN2", target_bir_lowering=False, num_devices=1)
    args = [nc.dram_tensor(n, a.shape, mybir.dt.from_np(a.dtype), kind="ExternalInput").ap() for n, a in arrays.items()]
    x_mid = nc.dram_tensor("x_mid", (P, KT, S), F32, kind="Internal").ap()
    sums = nc.dram_tensor("sums", (MLA_HEADS, S), F32, kind="Internal").ap()
    out = nc.dram_tensor("out", (P, KT, S), F32, kind="ExternalOutput").ap()
    build(nc, *args, x_mid, sums, out)
    res = run(nc, [arrays], core_ids=[0]).results[0]["out"]
    return np.ascontiguousarray(res.transpose(1, 0, 2).reshape(1, D, S).transpose(0, 2, 1))
```
